# Optimizing a Trainium2 kernel written in Bass

```python
import jax, jax.numpy as jnp
from jax import lax
import numpy as np
import math

D_MODEL = 2048
BATCH = 1
SEQ = 256
DEPTH = 1

ATT_HEADS = 16
ATT_KV_HEADS = 2
HEAD_DIM = 64
ATT_WIDTH = ATT_HEADS * HEAD_DIM
KV_WIDTH = ATT_KV_HEADS * HEAD_DIM
GROUP = ATT_HEADS // ATT_KV_HEADS
WINDOW = 128
BLOCK = 128
ROT_DIM = HEAD_DIM // 4
ROPE_THETA = 500000.0
HG_HEADS = 8
HG_EXPAND = 128
HG_HEAD_V = 128
HG_F_WIDTH = HG_HEADS * HG_EXPAND
HG_V_WIDTH = HG_HEADS * HG_HEAD_V
CHUNK = 64
N_LB = DEPTH + 1
FFN_HIDDEN = ((8 * D_MODEL // 3 + 255) // 256) * 256
N_MOD = 6
IN_COLS = ATT_WIDTH + 2 * KV_WIDTH + 2 * HG_F_WIDTH + 2 * HG_V_WIDTH + 2 * D_MODEL
EPS = 1e-6


def rmsnorm(t, gain):
    t32 = t.astype(jnp.float32)
    y = t32 * lax.rsqrt(jnp.mean(t32 * t32, axis=-1, keepdims=True) + EPS)
    return (y * gain.astype(jnp.float32)).astype(t.dtype)

def rope_partial(t, cos, sin):
    half = ROT_DIM // 2
    t1 = t[..., :half].astype(jnp.float32)
    t2 = t[..., half:ROT_DIM].astype(jnp.float32)
    rot = jnp.concatenate([t1 * cos - t2 * sin, t2 * cos + t1 * sin], axis=-1)
    return jnp.concatenate([rot.astype(t.dtype), t[..., ROT_DIM:]], axis=-1)

def sliding_window_attention(q, k, v, sinks):
    B, S = q.shape[0], q.shape[1]
    nb = S // BLOCK
    qb = q.reshape(B, nb, BLOCK, ATT_KV_HEADS, GROUP, HEAD_DIM).astype(jnp.float32)
    kb = k.reshape(B, nb, BLOCK, ATT_KV_HEADS, HEAD_DIM).astype(jnp.float32)
    vb = v.reshape(B, nb, BLOCK, ATT_KV_HEADS, HEAD_DIM).astype(jnp.float32)
    prev = lambda t: jnp.concatenate([jnp.zeros_like(t[:, :1]), t[:, :-1]], axis=1)
    kk = jnp.concatenate([prev(kb), kb], axis=2)
    vv = jnp.concatenate([prev(vb), vb], axis=2)
    logits = jnp.einsum('bnqhgd,bnkhd->bnhgqk', qb, kk) * (HEAD_DIM ** -0.5)
    qi = jnp.arange(BLOCK)[:, None]
    kj = jnp.arange(2 * BLOCK)[None, :]
    rel = BLOCK + qi - kj
    band = (rel >= 0) & (rel < WINDOW)
    has_prev = (jnp.arange(nb) > 0)[:, None, None] | (kj >= BLOCK)[None]
    mask = band[None] & has_prev
    logits = jnp.where(mask[None, :, None, None], logits, -jnp.inf)
    sink = sinks.astype(jnp.float32).reshape(ATT_KV_HEADS, GROUP)[None, None, :, :, None, None]
    m = jnp.maximum(jnp.max(logits, axis=-1, keepdims=True), sink)
    p = jnp.exp(logits - m)
    denom = jnp.sum(p, axis=-1, keepdims=True) + jnp.exp(sink - m)
    out = jnp.einsum('bnhgqk,bnkhd->bnqhgd', p / denom, vv)
    return out.reshape(B, S, ATT_WIDTH).astype(q.dtype)

def hgrn2_recurrence(q, f_raw, i, lb):
    B, S = q.shape[0], q.shape[1]
    nc = S // CHUNK
    f = lb + (1.0 - lb) * jax.nn.sigmoid(f_raw.astype(jnp.float32))
    key = 1.0 - f
    logf = jnp.log(f)

    def chunks(t, d):
        return t.astype(jnp.float32).reshape(B, nc, CHUNK, HG_HEADS, d).transpose(1, 0, 3, 2, 4)

    qc = chunks(jax.nn.silu(q.astype(jnp.float32)), HG_EXPAND)
    kc = chunks(key, HG_EXPAND)
    vc = chunks(i, HG_HEAD_V)
    bc = jnp.cumsum(chunks(logf, HG_EXPAND), axis=3)
    causal = jnp.tril(jnp.ones((CHUNK, CHUNK), dtype=bool))[:, :, None]

    def step(state, xs):
        qt, kt, vt, bt = xs
        o_inter = jnp.einsum('bhck,bhkv->bhcv', qt * jnp.exp(bt), state)
        diff = bt[:, :, :, None, :] - bt[:, :, None, :, :]
        decay = jnp.where(causal, jnp.exp(jnp.where(causal, diff, 0.0)), 0.0)
        scores = jnp.einsum('bhtk,bhtsk,bhsk->bhts', qt, decay, kt)
        o = o_inter + jnp.einsum('bhts,bhsv->bhtv', scores, vt)
        b_last = bt[:, :, -1:, :]
        new_state = (jnp.exp(b_last[:, :, 0, :])[..., None] * state
                     + jnp.einsum('bhsk,bhsv->bhkv', kt * jnp.exp(b_last - bt), vt))
        return new_state, o

    state0 = jnp.zeros((B, HG_HEADS, HG_EXPAND, HG_HEAD_V), jnp.float32)
    _, o = lax.scan(step, state0, (qc, kc, vc, bc))
    return o.transpose(1, 0, 3, 2, 4).reshape(B, S, HG_HEADS, HG_HEAD_V)

def first_inputs(seed: int = 0) -> dict:
    key = jax.random.key(seed)
    ks = jax.random.split(key, 20)
    f32 = jnp.float32
    nrm = lambda k, shape, scale: (jax.random.normal(k, shape, f32) * scale)
    gain = lambda k, shape: 1.0 + 0.05 * jax.random.normal(k, shape, f32)
    offsets = jax.random.randint(ks[2], (BATCH, 1), 0, 4096, dtype=jnp.int32)
    positions = (offsets + jnp.arange(SEQ, dtype=jnp.int32)[None, :]).astype(jnp.int32)
    return {
        "x": nrm(ks[0], (BATCH, SEQ, D_MODEL), 1.0),
        "c": nrm(ks[1], (BATCH, D_MODEL), 1.0),
        "positions": positions,
        "w_ada": nrm(ks[3], (DEPTH, D_MODEL, N_MOD * D_MODEL), 0.5 * D_MODEL ** -0.5),
        "b_ada": nrm(ks[4], (DEPTH, N_MOD * D_MODEL), 0.02),
        "g_pre_mix": gain(ks[5], (DEPTH, D_MODEL)),
        "g_post_mix": gain(ks[6], (DEPTH, D_MODEL)),
        "g_pre_ffn": gain(ks[7], (DEPTH, D_MODEL)),
        "g_post_ffn": gain(ks[8], (DEPTH, D_MODEL)),
        "w_in": nrm(ks[9], (DEPTH, D_MODEL, IN_COLS), D_MODEL ** -0.5),
        "attn_sinks": nrm(ks[10], (DEPTH, ATT_HEADS), 1.0),
        "w_attn_proj": nrm(ks[11], (DEPTH, ATT_WIDTH, D_MODEL), ATT_WIDTH ** -0.5),
        "hg_lower_bounds": nrm(ks[12], (N_LB, HG_F_WIDTH), 0.5),
        "hg_norm": gain(ks[13], (DEPTH, HG_HEAD_V)),
        "w_hgrn_proj": nrm(ks[14], (DEPTH, HG_V_WIDTH, D_MODEL), HG_V_WIDTH ** -0.5),
        "w_out": nrm(ks[15], (DEPTH, D_MODEL, D_MODEL), D_MODEL ** -0.5),
        "w_ffn_in": nrm(ks[16], (DEPTH, D_MODEL, 2 * FFN_HIDDEN), D_MODEL ** -0.5),
        "w_ffn_out": nrm(ks[17], (DEPTH, FFN_HIDDEN, D_MODEL), FFN_HIDDEN ** -0.5),
    }

def first_block(x, c, positions, w_ada, b_ada, g_pre_mix, g_post_mix, g_pre_ffn, g_post_ffn,
              w_in, attn_sinks, w_attn_proj, hg_lower_bounds, hg_norm, w_hgrn_proj, w_out,
              w_ffn_in, w_ffn_out):
    B, S = x.shape[0], x.shape[1]
    inv_freq = ROPE_THETA ** (-jnp.arange(0, ROT_DIM, 2, dtype=jnp.float32) / ROT_DIM)
    ang = positions.astype(jnp.float32)[..., None] * inv_freq
    cos, sin = jnp.cos(ang)[:, :, None, :], jnp.sin(ang)[:, :, None, :]
    lb_table = jnp.cumsum(jax.nn.softmax(hg_lower_bounds.astype(jnp.float32), axis=0), axis=0)
    splits = [ATT_WIDTH, ATT_WIDTH + KV_WIDTH, ATT_WIDTH + 2 * KV_WIDTH,
              ATT_WIDTH + 2 * KV_WIDTH + HG_F_WIDTH,
              ATT_WIDTH + 2 * KV_WIDTH + 2 * HG_F_WIDTH,
              ATT_WIDTH + 2 * KV_WIDTH + 2 * HG_F_WIDTH + HG_V_WIDTH,
              ATT_WIDTH + 2 * KV_WIDTH + 2 * HG_F_WIDTH + 2 * HG_V_WIDTH,
              ATT_WIDTH + 2 * KV_WIDTH + 2 * HG_F_WIDTH + 2 * HG_V_WIDTH + D_MODEL]
    for l in range(DEPTH):
        mod = (c @ w_ada[l] + b_ada[l])[:, None, :]
        shift1, scale1, gate1, shift2, scale2, gate2 = jnp.split(mod, N_MOD, axis=-1)

        h = rmsnorm(x, g_pre_mix[l]) * (1.0 + scale1) + shift1
        proj = h @ w_in[l]
        q_a, k_a, v_a, q_h, f_h, i_h, g_h, gate_a, gate_h = jnp.split(proj, splits, axis=-1)
        qa = rope_partial(q_a.reshape(B, S, ATT_HEADS, HEAD_DIM), cos, sin)
        ka = rope_partial(k_a.reshape(B, S, ATT_KV_HEADS, HEAD_DIM), cos, sin)
        va = v_a.reshape(B, S, ATT_KV_HEADS, HEAD_DIM)
        y_a = sliding_window_attention(qa, ka, va, attn_sinks[l]) @ w_attn_proj[l]
        o_h = hgrn2_recurrence(q_h, f_h, i_h, lb_table[l])
        o_h = rmsnorm(o_h, hg_norm[l]).reshape(B, S, HG_V_WIDTH).astype(x.dtype)
        y_h = (o_h * jax.nn.sigmoid(g_h)) @ w_hgrn_proj[l]
        merged = jax.nn.sigmoid(gate_a) * y_a + jax.nn.sigmoid(gate_h) * y_h
        y = merged @ w_out[l]
        x = x + gate1 * rmsnorm(y, g_post_mix[l])

        h = rmsnorm(x, g_pre_ffn[l]) * (1.0 + scale2) + shift2
        gu = h @ w_ffn_in[l]
        g_ffn, u_ffn = jnp.split(gu, 2, axis=-1)
        y = (jax.nn.silu(g_ffn) * u_ffn) @ w_ffn_out[l]
        x = x + gate2 * rmsnorm(y, g_post_ffn[l])
    return x


MIX_WIDTH = D_MODEL
HEAD_DIM_2 = 128
ATTN_WIDTH = MIX_WIDTH // 2
ATTN_HEADS = ATTN_WIDTH // HEAD_DIM_2
POOL_WIDTH = MIX_WIDTH - ATTN_WIDTH
POOL_WINDOWS = (2, 4, 8, 16)
POOL_GROUPS = len(POOL_WINDOWS)
POOL_GROUP_WIDTH = POOL_WIDTH // POOL_GROUPS
IN_WIDTH = 3 * ATTN_WIDTH + POOL_WIDTH
MOBA_BLOCK = 256
MOBA_TOPK = 3
Q_CHUNK = 64
REL_BUCKETS = 32
REL_MAX_DIST = 1024
D_FF = 256 * ((8 * D_MODEL // 3 + 255) // 256)
CONV_WIDTH = 3
NEG = -1e30


def rms_norm(x, g):
    xf = x.astype(jnp.float32)
    y = xf * lax.rsqrt(jnp.mean(xf * xf, axis=-1, keepdims=True) + EPS)
    return (y * g.astype(jnp.float32)).astype(x.dtype)

def rel_bucket(dist):
    n = jnp.maximum(dist, 0)
    max_exact = REL_BUCKETS // 2
    nf = jnp.maximum(n, max_exact).astype(jnp.float32)
    large = max_exact + (jnp.log(nf / max_exact) / math.log(REL_MAX_DIST / max_exact)
                         * (REL_BUCKETS - max_exact)).astype(jnp.int32)
    large = jnp.minimum(large, REL_BUCKETS - 1)
    return jnp.where(n < max_exact, n, large)

def moba_attention(q, k, v, rel_bias):
    B, H, S, Dh = q.shape
    nb = -(-S // MOBA_BLOCK)
    S_pad = nb * MOBA_BLOCK
    pad = ((0, 0), (0, 0), (0, S_pad - S), (0, 0))
    q, k, v = jnp.pad(q, pad), jnp.pad(k, pad), jnp.pad(v, pad)
    K = min(MOBA_TOPK, nb)
    kb = k.reshape(B, H, nb, MOBA_BLOCK, Dh)
    vb = v.reshape(B, H, nb, MOBA_BLOCK, Dh)
    k_mean = jnp.mean(kb.astype(jnp.float32), axis=3)
    gate = jnp.einsum('bhsd,bhnd->bhsn', q.astype(jnp.float32), k_mean)
    q_blk = jnp.arange(S_pad) // MOBA_BLOCK
    past = jnp.arange(nb)[None, :] < q_blk[:, None]
    gate = jnp.where(past, gate, NEG)
    _, sel = lax.top_k(gate, K)
    n_chunks = S_pad // Q_CHUNK
    sel_chunks = sel.reshape(B, H, n_chunks, Q_CHUNK, K).transpose(2, 0, 1, 3, 4)
    b_idx = jnp.arange(B)[:, None, None, None]
    h_idx = jnp.arange(H)[None, :, None, None]
    offs = jnp.arange(MOBA_BLOCK)
    scale = Dh ** -0.5

    def chunk(args):
        c, sel_c = args
        q0 = c * Q_CHUNK
        own = q0 // MOBA_BLOCK
        qc = lax.dynamic_slice_in_dim(q, q0, Q_CHUNK, axis=2)
        q_pos = q0 + jnp.arange(Q_CHUNK)
        k_sel = kb[b_idx, h_idx, sel_c]
        v_sel = vb[b_idx, h_idx, sel_c]
        s_sel = jnp.einsum('bhqd,bhqnkd->bhqnk', qc, k_sel).astype(jnp.float32) * scale
        kpos_sel = sel_c[..., None] * MOBA_BLOCK + offs
        bias_sel = rel_bias[h_idx[..., None], rel_bucket(q_pos[:, None, None] - kpos_sel)]
        valid = (sel_c < own)[..., None]
        s_sel = jnp.where(valid, s_sel + bias_sel.astype(jnp.float32), NEG)
        s_sel = s_sel.reshape(B, H, Q_CHUNK, K * MOBA_BLOCK)
        k_own = lax.dynamic_index_in_dim(kb, own, axis=2, keepdims=False)
        v_own = lax.dynamic_index_in_dim(vb, own, axis=2, keepdims=False)
        s_own = jnp.einsum('bhqd,bhkd->bhqk', qc, k_own).astype(jnp.float32) * scale
        dist_own = q_pos[:, None] - (own * MOBA_BLOCK + offs)[None, :]
        bias_own = rel_bias[:, rel_bucket(dist_own)].astype(jnp.float32)
        s_own = jnp.where(dist_own >= 0, s_own + bias_own, NEG)
        probs = jax.nn.softmax(jnp.concatenate([s_sel, s_own], axis=-1), axis=-1)
        p_sel = probs[..., :K * MOBA_BLOCK].reshape(
            B, H, Q_CHUNK, K, MOBA_BLOCK).astype(v.dtype)
        p_own = probs[..., K * MOBA_BLOCK:].astype(v.dtype)
        return (jnp.einsum('bhqnk,bhqnkd->bhqd', p_sel, v_sel)
                + jnp.einsum('bhqk,bhkd->bhqd', p_own, v_own))

    outs = lax.map(chunk, (jnp.arange(n_chunks), sel_chunks))
    out = outs.transpose(1, 0, 3, 2, 4).reshape(B, S_pad, H * Dh)
    return out[:, :S]

def multiscale_pool(p, pool_w, pool_scale):
    B, S, C = p.shape
    pf = p.astype(jnp.float32)
    csum = jnp.concatenate([jnp.zeros((B, 1, C), jnp.float32), jnp.cumsum(pf, axis=1)], axis=1)
    t = jnp.arange(S)
    outs = []
    for g, w in enumerate(POOL_WINDOWS):
        sl = slice(g * POOL_GROUP_WIDTH, (g + 1) * POOL_GROUP_WIDTH)
        cg = csum[:, :, sl]
        start = jnp.maximum(t + 1 - w, 0)
        count = jnp.minimum(t + 1, w).astype(jnp.float32)[None, :, None]
        mixed = (cg[:, 1:] - cg[:, start]) / count - pf[:, :, sl]
        outs.append(jnp.einsum('bsc,cd->bsd', mixed.astype(p.dtype), pool_w[g]))
    return jnp.concatenate(outs, axis=-1) * pool_scale

def conv_ffn(h, w_up, conv_w, conv_b, w_down):
    u = h @ w_up
    S = u.shape[1]
    u_pad = jnp.pad(u, ((0, 0), (CONV_WIDTH - 1, 0), (0, 0)))
    y = conv_b
    for i in range(CONV_WIDTH):
        y = y + conv_w[i] * u_pad[:, i:i + S]
    gate, val = jnp.split(y, 2, axis=-1)
    return (jax.nn.silu(gate) * val) @ w_down

def second_inputs(seed: int = 0) -> dict:
    key = jax.random.key(seed)
    ks = jax.random.split(key, 16)
    f32 = jnp.float32
    nrm = lambda k, shape, s: jax.random.normal(k, shape, f32) * s
    return {
        'x': nrm(ks[0], (BATCH, SEQ, D_MODEL), 1.0),
        'attn_norm_g': 1.0 + nrm(ks[1], (DEPTH, D_MODEL), 0.02),
        'w_in': nrm(ks[2], (DEPTH, D_MODEL, IN_WIDTH), D_MODEL ** -0.5),
        'q_norm_g': 1.0 + nrm(ks[3], (DEPTH, HEAD_DIM_2), 0.02),
        'k_norm_g': 1.0 + nrm(ks[4], (DEPTH, HEAD_DIM_2), 0.02),
        'rel_bias': nrm(ks[5], (ATTN_HEADS, REL_BUCKETS), 0.5),
        'pool_w': nrm(ks[6], (DEPTH, POOL_GROUPS, POOL_GROUP_WIDTH, POOL_GROUP_WIDTH), POOL_GROUP_WIDTH ** -0.5),
        'pool_scale': 1.0 + nrm(ks[7], (DEPTH, POOL_WIDTH), 0.1),
        'w_out': nrm(ks[8], (DEPTH, MIX_WIDTH, D_MODEL), MIX_WIDTH ** -0.5),
        'ffn_norm_g': 1.0 + nrm(ks[9], (DEPTH, D_MODEL), 0.02),
        'w_up': nrm(ks[10], (DEPTH, D_MODEL, 2 * D_FF), D_MODEL ** -0.5),
        'conv_w': nrm(ks[11], (DEPTH, CONV_WIDTH, 2 * D_FF), CONV_WIDTH ** -0.5),
        'conv_b': nrm(ks[12], (DEPTH, 2 * D_FF), 0.01),
        'w_down': nrm(ks[13], (DEPTH, D_FF, D_MODEL), D_FF ** -0.5),
    }

def second_block(x, attn_norm_g, w_in, q_norm_g, k_norm_g, rel_bias, pool_w, pool_scale,
              w_out, ffn_norm_g, w_up, conv_w, conv_b, w_down):
    B, S, _ = x.shape

    def heads(t):
        return t.reshape(B, S, ATTN_HEADS, HEAD_DIM_2).transpose(0, 2, 1, 3)

    for l in range(DEPTH):
        h = rms_norm(x, attn_norm_g[l])
        proj = h @ w_in[l]
        q, k, v, p = jnp.split(proj, [ATTN_WIDTH, 2 * ATTN_WIDTH, 3 * ATTN_WIDTH], axis=-1)
        q = rms_norm(heads(q), q_norm_g[l])
        k = rms_norm(heads(k), k_norm_g[l])
        a = moba_attention(q, k, heads(v), rel_bias)
        m = multiscale_pool(p, pool_w[l], pool_scale[l])
        x = x + jnp.concatenate([a, m], axis=-1) @ w_out[l]
        x = x + conv_ffn(rms_norm(x, ffn_norm_g[l]), w_up[l], conv_w[l], conv_b[l], w_down[l])
    return x


def setup_inputs(seed=0):
    out = dict(first_inputs(seed))
    for name, value in second_inputs(seed + 1).items():
        if name != "x":
            out[name + "_2"] = value
    return out


def reference(
    x, c, positions, w_ada, b_ada, g_pre_mix, g_post_mix, g_pre_ffn, g_post_ffn, w_in,
    attn_sinks, w_attn_proj, hg_lower_bounds, hg_norm, w_hgrn_proj, w_out, w_ffn_in, w_ffn_out,
    attn_norm_g_2, w_in_2, q_norm_g_2, k_norm_g_2, rel_bias_2, pool_w_2, pool_scale_2, w_out_2,
    ffn_norm_g_2, w_up_2, conv_w_2, conv_b_2, w_down_2,
):
    x = first_block(
        x, c, positions, w_ada, b_ada, g_pre_mix, g_post_mix, g_pre_ffn, g_post_ffn, w_in,
        attn_sinks, w_attn_proj, hg_lower_bounds, hg_norm, w_hgrn_proj, w_out, w_ffn_in,
        w_ffn_out,
    )
    return second_block(
        x, attn_norm_g_2, w_in_2, q_norm_g_2, k_norm_g_2, rel_bias_2, pool_w_2, pool_scale_2,
        w_out_2, ffn_norm_g_2, w_up_2, conv_w_2, conv_b_2, w_down_2,
    )


_drawn_inputs = setup_inputs


def setup_inputs(seed=0):
    import zlib

    import numpy as np

    out = dict(_drawn_inputs(seed))
    spreads = {}
    factors = {'attn_sinks': 2.972,
     'hg_lower_bounds': 3.87,
     'hg_norm': 3.149,
     'attn_norm_g_2': 5.415,
     'q_norm_g_2': 8.0,
     'k_norm_g_2': 8.0,
     'ffn_norm_g_2': 4.986,
     'conv_b_2': 8.0}
    for name, (base, spread) in spreads.items():
        noise = np.random.default_rng([zlib.crc32(name.encode()), seed]).standard_normal(out[name].shape)
        drawn = base * np.exp(spread * noise) if base else spread * noise
        out[name] = __import__('jax').numpy.asarray(drawn.astype(out[name].dtype))
    for name, factor in factors.items():
        out[name] = (out[name] * factor).astype(out[name].dtype)
    return out
```

```python
import math
import numpy as np
import concourse.bass as bass
from concourse import mybir
from contextlib import ExitStack

F32 = mybir.dt.float32
R32 = mybir.dt.float32r
BF16 = mybir.dt.bfloat16
I32 = mybir.dt.int32
ALU = mybir.AluOpType
ACT = mybir.ActivationFunctionType
AX = mybir.AxisListType
ds = bass.ds

P = 128
S = 256
D = 2048
DT = D // P
HEADS1, KV1, HD1 = 16, 2, 64
ROT = HD1 // 4
THETA = 500000.0
HGH = 8
CH = 64
LEVELS = (32, 16, 8, 4, 2, 1)
HID = 5632
HIDT = HID // P
HEADS2 = 8
BUCKETS, MAX_DIST = 32, 1024
WINDOWS = (2, 4, 8, 16)
EPS = 1e-6
NEG = -1e30
TINY = 1e-19

KC = 4
CW = 256
RING = 4
ADA_CB = 1024

PAR = {}
_n = 0
for _name, _w in (("c", DT), ("b_ada", 6 * DT), ("g_pre_mix", DT), ("g_post_mix", DT), ("g_pre_ffn", DT),
                  ("g_post_ffn", DT), ("sinks", HEADS1), ("lb0", HGH), ("lb1", HGH), ("hg_norm", 1),
                  ("attn_norm_g_2", DT), ("q_norm_g_2", 1), ("k_norm_g_2", 1), ("pool_scale_2", 8),
                  ("ffn_norm_g_2", DT), ("conv_w_2", 3 * 2 * HIDT), ("conv_b_2", 2 * HIDT)):
    PAR[_name] = (_n, _n + _w)
    _n += _w
NPAR = _n

CON = {}
_n = 0
for _name, _w in (("ident", P), ("flip", P), ("rope_swap", P), ("kv_pick", 2 * P), ("level_mask", 8 * P),
                  ("inv_freq", 1), ("band_mask", 3 * P), ("inv_count", 4 * S), ("chunk_scan", S)):
    CON[_name] = (_n, _n + _w)
    _n += _w
NCON = _n
HANKEL_W = 3 * P


def constants():
    con = np.zeros((P, NCON), np.float32)
    p = np.arange(P)

    def put(name, a):
        con[:, CON[name][0]:CON[name][1]] = a.reshape(P, -1)

    put("ident", np.eye(P))
    put("flip", np.eye(P)[::-1])
    swap = np.zeros((P, P))
    half = ROT // 2
    for head in range(P // HD1):
        for d in range(half):
            swap[head * HD1 + d + half, head * HD1 + d] = -1.0
            swap[head * HD1 + d, head * HD1 + d + half] = 1.0
    put("rope_swap", swap)
    pick = np.zeros((P, 2, P))
    for g in range(2):
        pick[HD1 * g + p % HD1, g, p] = 1.0
    put("kv_pick", pick)
    s, t = p[:, None], p[None, :]
    mask = np.zeros((P, 8, P))
    for n, m in enumerate(LEVELS + (CH,)):
        mask[:, n] = (s // (2 * m) == t // (2 * m)) & (s % (2 * m) < m) & (t % (2 * m) >= m)
    mask[:, 7] = s == t
    put("level_mask", mask)
    freq = np.float32(THETA) ** (-np.arange(0, ROT, 2, dtype=np.float32) / np.float32(ROT))
    col = np.zeros((P, 1), np.float32)
    for head in range(P // HD1):
        for d in range(ROT):
            col[head * HD1 + d, 0] = freq[d % half]
    put("inv_freq", col)
    band = np.full((P, 3, P), NEG)
    band[:, 0][t <= s] = 0.0
    band[:, 1][t > s] = 0.0
    band[:, 2][t <= s] = 0.0
    put("band_mask", band)
    cnt = np.zeros((P, 4, S), np.float32)
    for g, w in enumerate(WINDOWS):
        cnt[:, g] = np.float32(1) / np.minimum(np.arange(S) + 1, w).astype(np.float32)
    put("inv_count", cnt)
    scan = np.ones((P, S))
    scan[:, ::CH] = 0.0
    put("chunk_scan", scan)
    dist = np.arange(S)
    exact = BUCKETS // 2
    far = np.maximum(dist, exact).astype(np.float32)
    large = exact + (np.log(far / np.float32(exact)) / np.float32(math.log(MAX_DIST / exact))
                     * np.float32(BUCKETS - exact)).astype(np.int32)
    bucket = np.where(dist < exact, dist, np.minimum(large, BUCKETS - 1))
    hot = np.zeros((BUCKETS, S), np.float32)
    hot[bucket[::-1], np.arange(S)] = 1.0
    return con, hot


class Job:

    def __init__(self, name, iters, groups):
        self.name, self.iters, self.groups = name, iters, groups
        self.chunks = [g[2] // KC for g in groups]
        self.offs = [sum(self.chunks[:n]) for n in range(len(groups))]
        self.per = sum(self.chunks)
        assert iters == 1 or (self.per % RING == 0 and len(groups) % 2 == 0)


def two_block_kernel(nc, xT, params, cons, hot_in, rel_bias, pos, w_ada, w_in, w_attn, w_hgrn, w_out,
                     w_ffn_in, w_ffn_out, w_in2, pool_w, w_out2, w_up, w_down, out, stop_after=None, taps=None):
    ACT_ = ACT
    ctx = ExitStack()
    with ctx:
        base = (nc.sbuf_base + 31) // 32 * 32
        ctx.enter_context(nc.sbuf_tensor("arena", [P, (nc.sbuf_usable_end - base - 64) // 4], F32))
        limit = nc.sbuf_usable_end
        cursor = [base]

        def place(name, shape, dt=F32, at=None):
            size = int(np.prod(shape[1:])) * (2 if dt == BF16 else 4)
            start = cursor[0] if at is None else at
            if at is None:
                cursor[0] = start + (size + 31) // 32 * 32
            assert start + size <= limit, (name, start + size - limit)
            return nc.alloc_sbuf_tensor_at(name, shape, dt, offset=start)

        par = place("par", [P, NPAR])
        con = place("con", [P, NCON])
        ones = place("ones", [P, P])
        ident_bf = place("ident_bf", [P, P], BF16)
        band_bf = place("band_bf", [P, 3 * P], BF16)
        mod = place("mod", [P, 6 * DT])
        coef = place("coef", [P, 4, DT])
        eps_col = place("eps_col", [P, 2])
        rstd = place("rstd", [P, S])
        lnv = place("lnv", [P, S])
        raw = place("raw", [P, RING, KC, CW])
        w_hi = place("w_hi", [P, RING, KC, CW], R32)
        w_lo = place("w_lo", [P, RING, KC, CW], R32)
        half = place("half", [P, 2, 2, CW])
        X = place("X", [P, DT, 2 * S], R32)
        mx, mx1, negm, den, es = [place(n, [P, 2, 4]) for n in ("mx", "mx1", "negm", "den", "es")]
        lbc = place("lbc", [P, 6, HGH])
        REG = cursor[0]
        KB = 1024

        ada_acc = place("ada_acc", [P, 2, 2, ADA_CB], at=REG)
        x1 = place("x1", [P, DT, S], at=REG + 16 * KB)
        sq1 = place("sq1", [P, DT, S], at=REG + 32 * KB)
        NP1 = 42
        proj = place("proj", [P, NP1, S], at=REG)
        QA, KA, VA, QH, FH, IH, GH = 0, 8, 9, 10, 18, 26, 34
        T0 = REG + NP1 * KB
        T1 = T0 + 29 * KB
        attn_x = place("attn_x", [P, 8, 2 * S], R32, at=T1)
        hgrn_x = place("hgrn_x", [P, 8, 2 * S], R32, at=T1 + 16 * KB)
        def seq(at, *items):
            outs = []
            for name, shape, dt in items:
                outs.append(place(name, shape, dt, at=at))
                at += (int(np.prod(shape[1:])) * 4 + 31) // 32 * 32
            return outs
        (pos_i, ang, turn, red, cosk, sink_, cosq, sinq, kr, kdup, v_sb, qr) = seq(
            T0, ("pos_i", [P, S], I32), ("ang", [P, S], F32), ("turn", [P, S], F32), ("red", [P, S], F32),
            ("cosk", [P, S], F32), ("sink_", [P, S], F32), ("cosq", [P, S], F32), ("sinq", [P, S], F32),
            ("kr", [P, S], F32), ("kdup", [P, 2, S], F32), ("v_sb", [P, 2, P], F32),
            ("qr", [P, 2, S], F32))
        (q_cos, q_sin) = seq(T0, ("q_cos", [P, 2, S], F32), ("q_sin", [P, 2, S], F32))
        (probs, probs_t) = seq(T0 + 14 * KB, ("probs", [P, 4, 3 * P], F32), ("probs_t", [P, 4, 3 * P], F32))
        (decay, Pq, Rk, hg_q, hg_k, hg_v, v_rows, s_ab, s_c, p_c, r_c) = seq(
            T0, ("decay", [P, 8, S], F32), ("Pq", [P, 7, S], F32), ("Rk", [P, 7, S], F32), ("hg_q", [P, S], F32),
            ("hg_k", [P, S], F32), ("hg_v", [P, S], F32), ("v_rows", [P, 2, P], F32), ("s_ab", [P, 2, P], F32),
            ("s_c", [P, P], F32), ("p_c", [P, P], F32), ("r_c", [P, P], F32))
        hg_l = lnv
        masked = place("masked", [P, 8, P], at=T0)
        hsq = place("hsq", [P, 8, S], at=T0)
        hrs = place("hrs", [P, 8, S], at=T0 + 8 * KB)
        hfull = place("hfull", [P, 8, S], at=T0 + 16 * KB)
        merged = place("merged", [P, DT, 2 * S], R32, at=REG)
        (t_a, t_h, sg_a, sg_h, u_a, u_h, full) = seq(
            T0, *[(n, [P, 2, CW], F32) for n in ("t_a", "t_h", "sg_a", "sg_h", "u_a", "u_h", "full")])
        x_res = place("x_res", [P, DT, S], at=REG + 86 * KB)
        y = place("y", [P, DT, S], at=REG + 70 * KB)
        hid = place("hid", [P, 24, 2 * S], R32, at=REG)
        sq = place("sq", [P, DT, S], at=REG + 48 * KB)
        (t_g, sg, t_u, fullf) = seq(REG + 48 * KB, *[(n, [P, 2, CW], F32) for n in ("t_g", "sg", "t_u", "fullf")])
        (cu, cacc, csg, cful) = seq(REG + 48 * KB, ("cu", [P, 2, 2, CW + 2], F32), ("cacc", [P, 2, 2, CW], F32),
                                    ("csg", [P, 2, CW], F32), ("cful", [P, 2, CW], F32))
        proj2 = place("proj2", [P, 32, S], at=REG)
        Q2, K2, V2, P2 = 0, 8, 16, 24
        v2_rows = place("v2_rows", [P, 2, 8, P], at=REG + 32 * KB)
        hank = place("hank", [P, 8, S], at=REG + 40 * KB)
        (probs2, probs2_t) = seq(REG + 48 * KB, ("probs2", [P, 4, 3 * P], F32), ("probs2_t", [P, 4, 3 * P], F32))
        sq2 = place("sq2", [P, DT, S], at=REG + 60 * KB)
        (bias_row, hot, relb, mx2, negm2, den2) = seq(REG + 76 * KB, ("bias_row", [P, HANKEL_W], F32), ("hot", [P, S], F32),
                                              ("relb", [P, HEADS2], F32), ("mx2", [P, 2, 4], F32),
                                              ("negm2", [P, 2, 4], F32), ("den2", [P, 2, 4], F32))
        PW = S + 16
        (pa, pb_, pc) = seq(REG + 32 * KB, *[(n, [P, 8, PW], F32) for n in ("pa", "pb_", "pc")])
        pwt = place("pwt", [P, 4, 2, S], at=REG + 60 * KB)
        pmix = place("pmix", [P, 8, S], at=REG + 68 * KB)
        pful = place("pful", [P, 8, S], at=REG + 76 * KB)
        hank_dram = nc.dram_tensor("hank_dram", (HEADS2, HANKEL_W), F32, kind="Internal")

        psg = ctx.enter_context(nc.psum_tensor("psg", [P, 4, 512], F32))
        pss = ctx.enter_context(nc.psum_tensor("pss", [P, 4, 512], F32))

        def sem(name):
            return ctx.enter_context(nc.semaphore(name))

        landed = [sem(f"landed{n}") for n in range(RING)]
        raw_used = sem("raw_used")
        hi_ready = sem("hi_ready")
        pe_chunk = sem("pe_chunk")
        half_ready = sem("half_ready")
        ps_free = sem("ps_free")
        par_in, con_in, x_in, misc_in = sem("par_in"), sem("con_in"), sem("x_in"), sem("misc_in")
        ones_set = sem("ones_set")
        x_back = sem("x_back")
        ada_mm, ada_out = sem("ada_mm"), sem("ada_out")
        dve_chain = sem("dve_chain")
        act_chain = sem("act_chain")
        act_parted, sp_parted = sem("act_parted"), sem("sp_parted")
        gate_ready, full_ready, fhi_ready, opnd_ready = sem("gate_ready"), sem("full_ready"), sem("fhi_ready"), sem("opnd_ready")
        sq_ready, ss_ready, rs_ready, nrm_full, nrm_hi, nrm_out = [sem(n) for n in
            ("sq_ready", "ss_ready", "rs_ready", "nrm_full", "nrm_hi", "nrm_out")]
        y_ready = sem("y_ready")
        out_done = sem("out_done")
        tap_done = sem("tap_done")
        S1 = {n: sem("a1_" + n) for n in ("trig", "tab", "swap", "kr", "dup", "dupo", "vt", "vo", "qswap", "qr",
                                          "s", "mx", "e", "es", "pn", "pt", "pto", "pv", "hi", "lo")}
        SH = {n: sem("hg_" + n) for n in ("act", "prep", "ln", "cp", "d", "exp", "pr", "vt", "vo", "sa", "sb", "ma", "mb",
                                          "sc", "sco", "o", "oo", "sq", "ss", "rs", "full", "hi", "lo", "lbm", "lbe")}
        S2 = {n: sem("a2_" + n) for n in ("sq", "ss", "rs", "qk", "vt", "vo", "row", "rowo", "dr", "hk", "s", "mx", "e",
                                          "pn", "pt", "pto", "pv", "hi", "lo", "mix", "pw", "pwm", "pfu", "phi", "plo")}
        local, hl, mul_done, add_done, cmid = [sem(n) for n in ("dve_local", "hg_local", "mul_done", "add_done", "cmid")]
        SC = {n: sem("cv_" + n) for n in ("zero", "aff", "acc")}

        def col(i, c0, step):
            return c0 + i * step

        def wide(W, k0, kt, c0, step=0):
            return (W.rearrange("(k p) n -> p k n", p=P), k0, kt, c0, step)

        GATE_A, GATE_H = NP1 * P, NP1 * P + D
        jobs = [
            Job("in0", 1, [wide(w_in, 0, DT, 0)]),
            Job("in", 10, [wide(w_in, 0, DT, CW, 2 * CW), wide(w_in, 0, DT, 2 * CW, 2 * CW)]),
            Job("merge", 8, [wide(w_in, 0, DT, GATE_A, CW), wide(w_attn, 0, 8, 0, CW),
                             wide(w_in, 0, DT, GATE_H, CW), wide(w_hgrn, 0, 8, 0, CW)]),
            Job("out", 4, [wide(w_out, 0, DT, 0, 2 * CW), wide(w_out, 0, DT, CW, 2 * CW)]),
            Job("up1a", 12, [wide(w_ffn_in, 0, DT, 0, CW), wide(w_ffn_in, 0, DT, HID, CW)]),
            Job("dn1a", 4, [wide(w_ffn_out, 0, 24, 0, 2 * CW), wide(w_ffn_out, 0, 24, CW, 2 * CW)]),
            Job("up1b", 10, [wide(w_ffn_in, 0, DT, 12 * CW, CW), wide(w_ffn_in, 0, DT, HID + 12 * CW, CW)]),
            Job("dn1b", 2, [wide(w_ffn_out, 24, 20, n * CW, 4 * CW) for n in range(4)]),
            Job("in2", 8, [wide(w_in2, 0, DT, 0, 2 * CW), wide(w_in2, 0, DT, CW, 2 * CW)]),
            Job("out2", 4, [wide(w_out2, 0, DT, 0, 2 * CW), wide(w_out2, 0, DT, CW, 2 * CW)]),
            Job("up2a", 12, [wide(w_up, 0, DT, 0, CW), wide(w_up, 0, DT, HID, CW)]),
            Job("dn2a", 4, [wide(w_down, 0, 24, 0, 2 * CW), wide(w_down, 0, 24, CW, 2 * CW)]),
            Job("up2b", 10, [wide(w_up, 0, DT, 12 * CW, CW), wide(w_up, 0, DT, HID + 12 * CW, CW)]),
            Job("dn2b", 2, [wide(w_down, 24, 20, n * CW, 4 * CW) for n in range(4)]),
        ]
        ADA_CHUNKS = (6 * D // ADA_CB) * DT
        r = ADA_CHUNKS
        G = 0
        for n, j in enumerate(jobs):
            j.r0, j.G0, j.next = r, G, jobs[n + 1] if n + 1 < len(jobs) else None
            r += j.iters * j.per
            G += j.iters * len(j.groups)
        J = {j.name: j for j in jobs}

        def chunk_no(j, i, g, c):
            return j.r0 + i * j.per + j.offs[g] + c

        def slot_of(j, g, c):
            return (j.r0 + j.offs[g] + c) % RING

        def landed_at(j, i, g, c):
            return 16 * ((j.r0 + j.offs[g] + c) // RING + 1) + i * (16 * j.per // RING)

        def group_no(j, i, g):
            return j.G0 + i * len(j.groups) + g

        def bank_of(j, g):
            return 2 * ((j.G0 + g) % 2)

        def chunks_done(j, i, g):
            return chunk_no(j, i, g, j.chunks[g]) - ADA_CHUNKS

        def is_static(v):
            return isinstance(v, int)

        def turns(eng, n, body):
            body(0)
            if n > 1:
                with eng.Fori(1, n) as i:
                    body(i)

        def tap(eng, k, src):
            if taps is not None:
                eng.dma_start(taps[k], src).then_inc(tap_done, 16)

        RUN = [j.name for j in jobs]
        if stop_after is not None:
            RUN = RUN[:RUN.index(stop_after) + 1] if stop_after in RUN else []
        live = [J[n] for n in RUN]
        for j in live:
            if j.next is not None and j.next.name not in RUN:
                j.next = None

        def runs(name):
            return name in RUN

        def flat3(a):
            return a.rearrange("p t s -> p (t s)")

        def flat(a):
            return flat3(a[:, :, :])

        block = ctx.enter_context(nc.Block())

        def P_(name, a=0, b=None):
            lo, hi = PAR[name]
            return par[:, lo + a:(hi if b is None else lo + b)]

        def C_(name, a=0, b=None):
            lo, hi = CON[name]
            return con[:, lo + a:(hi if b is None else lo + b)]

        @block.sync
        def _(sp):
            sp.dma_start(par[:, :], params).then_inc(par_in, 16)
            sp.dma_start(x1[:, :, :], xT.rearrange("(t p) s -> p t s", p=P)).then_inc(x_in, 16)
            sp.dma_start(con[:, :], cons).then_inc(con_in, 16)
            ada_v = w_ada.rearrange("(k p) n -> p k n", p=P)

            def ada_turn(i):
                for cb in range(2):
                    for k in range(DT):
                        n = cb * DT + k
                        if not (is_static(i) and n < RING):
                            sp.wait_ge(raw_used, i * 2 * DT + n - RING + 1)
                        sp.dma_start(raw[:, n % RING, :, :].rearrange("p k n -> p (k n)"),
                                     ada_v[:, k, ds(i * 2 * ADA_CB + cb * ADA_CB, ADA_CB)]
                                     ).then_inc(landed[n % RING], 16)
            turns(sp, 6 * D // ADA_CB // 2, ada_turn)

            def job_turn(j):
                def turn(i):
                    for g, (W, k0, kt, c0, step) in enumerate(j.groups):
                        for c in range(j.chunks[g]):
                            sp.wait_ge(raw_used, chunk_no(j, i, g, c) - RING + 1)
                            if not is_static(i):
                                sp.sem_inc(sp_parted, 1)
                            sp.dma_start(raw[:, slot_of(j, g, c), :, :],
                                         W[:, k0 + c * KC:k0 + (c + 1) * KC, ds(col(i, c0, step), CW)]
                                         ).then_inc(landed[slot_of(j, g, c)], 16)
                return turn
            for j in live:
                turns(sp, j.iters, job_turn(j))

        def bcast_rows(a):
            return bass.AP(tensor=a.tensor, offset=a.offset, ap=[[0, P], [1, S]])

        def shifted_rows(h):
            return bass.AP(tensor=h, offset=0, ap=[[1, P], [HANKEL_W, HEADS2], [1, S]])

        @block.gpsimd
        def _(pool):
            nt = 0
            if stop_after == "ada":
                pool.wait_ge(dve_chain, 2)
                tap(pool, 0, mod[:, :]); nt += 1
                pool.wait_ge(nrm_out, 4)
                tap(pool, 1, X[:, :, :].bitcast(F32).rearrange("p t s -> p (t s)")); nt += 1
            if runs("in"):
                pool.wait_ge(ps_free, J["in0"].G0 + 1)
                pool.dma_start(pos_i[:, :], bcast_rows(pos)).then_inc(misc_in, 16)
            if runs("out"):
                pool.wait_ge(pe_chunk, chunks_done(J["merge"], J["merge"].iters - 1, 3))
                pool.dma_start(x_res[:, :, :], xT.rearrange("(t p) s -> p t s", p=P)).then_inc(x_back, 16)
            if runs("in2"):
                pool.wait_ge(pe_chunk, chunks_done(J["dn1b"], 1, 3))
                pool.wait_ge(nrm_out, 12)
                pool.dma_start(hot[0:BUCKETS, :], hot_in).then_inc(misc_in, 16)
                pool.dma_start(relb[0:BUCKETS, :], rel_bias).then_inc(misc_in, 16)
                pool.wait_ge(S2["rowo"], 2)
                pool.dma_start(hank_dram.ap(), bias_row[0:HEADS2, :]).then_inc(S2["dr"], 16)
                pool.wait_ge(S2["dr"], 16)
                pool.dma_start(hank[:, :, :], shifted_rows(hank_dram)).then_inc(S2["hk"], 16)
                pool.wait_ge(S2["pto"], 2)
                pool.dma_start(pwt[:, :, :, :], pool_w.rearrange("g (k p) n -> p g k n", p=P)).then_inc(S2["pw"], 16)
            if taps is not None:
                if stop_after == "in":
                    pool.wait_ge(SH["lo"], 1)
                    tap(pool, 0, attn_x[:, :, :].bitcast(F32).rearrange("p t s -> p (t s)")); nt += 1
                    tap(pool, 1, hgrn_x[:, :, :].bitcast(F32).rearrange("p t s -> p (t s)")); nt += 1
                if stop_after in ("out", "dn1b", "dn1a", "in2", "out2"):
                    pool.wait_ge(y_ready, {"out": 1, "dn1a": 1, "dn1b": 2, "in2": 2, "out2": 2}[stop_after])
                    if stop_after == "out2":
                        pool.wait_ge(add_done, 16)
                    tap(pool, 0, x_res[:, :, :].rearrange("p t s -> p (t s)")); nt += 1
                    if stop_after == "in2":
                        pool.wait_ge(S2["plo"], 1)
                        tap(pool, 1, X[:, :, :].bitcast(F32).rearrange("p t s -> p (t s)")); nt += 1
                pool.wait_ge(tap_done, 16 * nt)
            if runs("dn2b"):
                for q in range(4):
                    pool.wait_ge(y_ready, 3 + q)
                    pool.dma_start(out.rearrange("(t p) s -> p t s", p=P)[:, 4 * q:4 * q + 4, :],
                                   x_res[:, 4 * q:4 * q + 4, :]).then_inc(out_done, 16)
                pool.wait_ge(out_done, 64)

        @block.scalar
        def _(act):
            chain = [0]

            def link(ins):
                ins.then_inc(act_chain, 1)
                chain[0] += 1
                act.wait_ge(act_chain, chain[0])

            def apart():
                act.sem_inc(act_parted, 1)

            def split(j, i, g, cs):
                for c in cs:
                    s = slot_of(j, g, c)
                    act.wait_ge(landed[s], landed_at(j, i, g, c))
                    if not (is_static(i) and chunk_no(j, i, g, c) - ADA_CHUNKS < RING):
                        act.wait_ge(pe_chunk, chunk_no(j, i, g, c) - ADA_CHUNKS - RING + 1)
                    nc.scalar.activation(w_hi[:, s, :, :], raw[:, s, :, :], ACT.Copy).then_inc(hi_ready, 1)

            def take_half(j, i, g):
                n, b = group_no(j, i, g), bank_of(j, g)
                act.wait_ge(pe_chunk, chunks_done(j, i, g))
                if not (is_static(i) and n < 2):
                    act.wait_ge(ps_free, n - 1)
                nc.scalar.activation(half[:, b // 2, :, :], psg[:, b:b + 2, CW:2 * CW], ACT.Copy).then_inc(half_ready, 1)

            def job(j, after=None, funcs=None):
                if funcs:
                    act.preload_act_table(funcs)
                split(j, 0, 0, range(RING, j.chunks[0]))

                def turn(i, last=False):
                    for g in range(len(j.groups)):
                        if g + 1 < len(j.groups):
                            split(j, i, g + 1, range(j.chunks[g + 1]))
                        elif not last:
                            split(j, i + 1, 0, range(j.chunks[0]))
                        elif j.next is not None:
                            split(j.next, 0, 0, range(min(RING, j.next.chunks[0])))
                        take_half(j, i, g)
                        if after:
                            after(i, g)
                if j.iters > 1:
                    with act.Fori(0, j.iters - 1) as i:
                        turn(i)
                turn(j.iters - 1, last=True)

            nrm = [0]

            def norm_stats(src, sqb, extra=None):
                k = nrm[0]
                for q in range(4):
                    if extra:
                        extra(q)
                    nc.scalar.activation(sqb[:, 4 * q:4 * q + 4, :], src[:, 4 * q:4 * q + 4, :], ACT.Square
                                         ).then_inc(sq_ready, 1)
                act.wait_ge(ss_ready, k + 1)
                link(nc.scalar.activation(lnv[:, :], pss[:, 0, 0:S], ACT.Ln, scale=1.0 / D, bias=eps_col[:, 0:1]))
                nc.scalar.activation(rstd[:, :], lnv[:, :], ACT.Exp, scale=-0.5).then_inc(rs_ready, 1)
                nrm[0] += 1

            opn = [0]

            def norm_operand(fullb):
                for q in range(4):
                    act.wait_ge(nrm_full, 4 * opn[0] + q + 1)
                    nc.scalar.activation(X[:, 4 * q:4 * q + 4, 0:S], fullb[:, 4 * q:4 * q + 4, :], ACT.Copy
                                         ).then_inc(nrm_hi, 1)
                opn[0] += 1

            act.wait_ge(ones_set, 1)
            norm_stats(x1, sq1, extra=lambda q: act.wait_ge(x_in, 16) if q == 0 else None)
            if live:
                split(J["in0"], 0, 0, range(RING))
            norm_operand(sq1)

            if runs("in"):
                job(J["in0"])
                job(J["in"])
                act.wait_ge(S1["trig"], 2)
                nc.scalar.activation(sink_[:, :], red[:, :], ACT.Sin).then_inc(S1["tab"], 1)
                nc.scalar.activation(cosk[:, :], turn[:, :], ACT.Sin).then_inc(S1["tab"], 1)
                nc.scalar.activation(proj[:, FH:FH + 8, :], proj[:, FH:FH + 8, :], ACT.Sigmoid).then_inc(SH["act"], 1)
                nc.scalar.activation(proj[:, GH:GH + 8, :], proj[:, GH:GH + 8, :], ACT.Sigmoid).then_inc(SH["act"], 1)
                nc.scalar.activation(proj[:, QH:QH + 8, :], proj[:, QH:QH + 8, :], ACT.Silu).then_inc(SH["act"], 1)
                act.wait_ge(S1["dup"], 2)
                nc.scalar.activation(kdup[:, :, :].rearrange("p a s -> p (a s)"), pss[:, 1, :], ACT.Copy).then_inc(S1["dupo"], 1)
                act.wait_ge(S1["vt"], 1)
                nc.scalar.activation(v_sb[:, :, :].rearrange("p a s -> p (a s)"), pss[:, 2, 0:S], ACT.Copy).then_inc(S1["vo"], 1)
                act.wait_ge(SH["lbm"], 1)
                nc.scalar.activation(lbc[:, 1:3, :], lbc[:, 1:3, :], ACT.Exp).then_inc(SH["lbe"], 1)
                for b in range(4):
                    act.wait_ge(S1["mx"], b + 1)
                    for hh in range(4):
                        nc.scalar.activation(probs[:, hh, 0:P], pss[:, hh, 0:P], ACT.Exp, bias=negm[:, 0, hh:hh + 1],
                                             accum_out=den[:, 0, hh:hh + 1])
                        nc.scalar.activation(probs[:, hh, P:3 * P], pss[:, hh, P:3 * P], ACT.Exp, bias=negm[:, 1, hh:hh + 1],
                                             accum_out=den[:, 1, hh:hh + 1]).then_inc(S1["e"], 1)
                    nc.scalar.activation(es[:, :, :], es[:, :, :], ACT.Exp).then_inc(S1["es"], 1)
                    act.wait_ge(S1["pt"], b + 1)
                    if b > 0:
                        act.wait_ge(S1["pv"], b)
                    nc.scalar.activation(probs_t[:, :, :], pss[:, :, 0:3 * P], ACT.Copy).then_inc(S1["pto"], 1)
                    act.wait_ge(S1["pv"], b + 1)
                    nc.scalar.activation(attn_x[:, 2 * b:2 * b + 2, 0:S], pss[:, 0, :].rearrange("p (a s) -> p a s", a=2),
                                         ACT.Copy).then_inc(S1["hi"], 1)
                act.preload_act_table_set("natural_log_exp_and_others")
                act.wait_ge(SH["prep"], 1)
                act.wait_ge(S1["lo"], 4)

                def head(h):
                    if not is_static(h):
                        act.wait_ge(SH["mb"], h)
                        apart()
                    nc.scalar.activation(hg_l[:, :], proj[:, ds(FH + h, 1), :].rearrange("p a s -> p (a s)"), ACT.Ln,
                                         bias=eps_col[:, 1:2]).then_inc(SH["ln"], 1)
                    nc.scalar.activation(hg_q[:, :], proj[:, ds(QH + h, 1), :].rearrange("p a s -> p (a s)"), ACT.Copy
                                         ).then_inc(SH["cp"], 1)
                    nc.scalar.activation(hg_v[:, :], proj[:, ds(IH + h, 1), :].rearrange("p a s -> p (a s)"), ACT.Copy
                                         ).then_inc(SH["cp"], 1)
                    act.wait_ge(SH["vt"], h + 1)
                    nc.scalar.activation(v_rows[:, :, :].rearrange("p a s -> p (a s)"), pss[:, 0, 0:S], ACT.Copy
                                         ).then_inc(SH["vo"], 1)
                    act.wait_ge(SH["d"], h + 1)
                    nc.scalar.activation(decay[:, :, :], decay[:, :, :], ACT.Exp).then_inc(SH["exp"], 1)
                    act.wait_ge(SH["sc"], h + 1)
                    nc.scalar.activation(s_c[:, :], pss[:, 0, 0:P], ACT.Copy).then_inc(SH["sco"], 1)
                    act.wait_ge(SH["o"], h + 1)
                    apart()
                    nc.scalar.activation(proj[:, ds(IH + h, 1), :].rearrange("p a s -> p (a s)"), pss[:, 2, 0:S], ACT.Copy
                                         ).then_inc(SH["oo"], 1)
                turns(act, HGH, head)
                act.wait_ge(SH["oo"], HGH)
                nc.scalar.activation(hsq[:, :, :], proj[:, IH:IH + 8, :], ACT.Square).then_inc(SH["sq"], 1)
                act.wait_ge(SH["ss"], 1)
                link(nc.scalar.activation(hrs[:, :, :].rearrange("p t s -> p (t s)"), pss[:, :, :].rearrange("p t s -> p (t s)"),
                                          ACT.Ln, scale=1.0 / P, bias=eps_col[:, 0:1]))
                nc.scalar.activation(hrs[:, :, :], hrs[:, :, :], ACT.Exp, scale=-0.5).then_inc(SH["rs"], 1)
                act.wait_ge(SH["full"], 1)
                nc.scalar.activation(hgrn_x[:, :, 0:S], hfull[:, :, :], ACT.Copy).then_inc(SH["hi"], 1)

            if runs("merge"):
                def after(i, g):
                    n = group_no(J["merge"], i, g)
                    if g in (0, 2):
                        act.wait_ge(ps_free, n + 1)
                        nc.scalar.activation((sg_a if g == 0 else sg_h)[:, :, :], (t_a if g == 0 else t_h)[:, :, :],
                                             ACT.Sigmoid).then_inc(gate_ready, 1)
                    if g == 3:
                        act.wait_ge(full_ready, i + 1)
                        apart()
                        nc.scalar.activation(merged[:, ds(2 * i, 2), 0:S], full[:, :, :], ACT.Copy).then_inc(fhi_ready, 1)
                job(J["merge"], after, ACT.Sigmoid)

            def swiglu_after(j, tb, sb, fb, k0):
                def after(i, g):
                    if g == 0:
                        act.wait_ge(ps_free, group_no(j, i, g) + 1)
                        nc.scalar.activation(sb[:, :, :], tb[:, :, :], ACT.Silu).then_inc(gate_ready, 1)
                    else:
                        act.wait_ge(full_ready, k0 + i + 1)
                        apart()
                        nc.scalar.activation(hid[:, ds(2 * i, 2), 0:S], fb[:, :, :], ACT.Copy).then_inc(fhi_ready, 1)
                return after

            def conv_after(j, k0):
                def after(i, g):
                    act.wait_ge(ps_free, group_no(j, i, g) + 1)
                    apart()
                    t0 = (24 if j.name == "up2b" else 0) + (HIDT if g else 0)
                    for a in range(2):
                        o = PAR["conv_w_2"][0] + 2 * 2 * HIDT + t0 + a
                        ob = PAR["conv_b_2"][0] + t0 + a
                        nc.scalar.activation(cacc[:, g, a, :], cu[:, g, a, 2:], ACT.Identity,
                                             scale=par[:, ds(2 * i + o, 1)], bias=par[:, ds(2 * i + ob, 1)]
                                             ).then_inc(SC["aff"], 1)
                    if g == 0:
                        act.wait_ge(SC["acc"], 2 * (k0 + i) + 1)
                        nc.scalar.activation(csg[:, :, :], cacc[:, 0, :, :], ACT.Silu).then_inc(gate_ready, 1)
                    else:
                        act.wait_ge(full_ready, 30 + k0 + i + 1)
                        apart()
                        nc.scalar.activation(hid[:, ds(2 * i, 2), 0:S], cful[:, :, :], ACT.Copy).then_inc(fhi_ready, 1)
                return after

            if runs("out"):
                job(J["out"])
                act.wait_ge(ps_free, J["up1a"].G0)
                norm_stats(y, sq)
                act.wait_ge(y_ready, 1)
                norm_stats(x_res, sq)
                norm_operand(sq)
            if runs("up1a"):
                job(J["up1a"], swiglu_after(J["up1a"], t_g, sg, fullf, 8), ACT.Silu)
                job(J["dn1a"])
                job(J["up1b"], swiglu_after(J["up1b"], t_g, sg, fullf, 20), ACT.Silu)
                job(J["dn1b"])
                act.wait_ge(add_done, 8)
                norm_stats(y, sq)
                act.wait_ge(y_ready, 2)
                norm_stats(x_res, sq)
                norm_operand(sq)

            if runs("in2"):
                job(J["in2"])
                act.wait_ge(ps_free, J["out2"].G0)
                for q in range(4):
                    nc.scalar.activation(sq2[:, 4 * q:4 * q + 4, :], proj2[:, 4 * q:4 * q + 4, :], ACT.Square).then_inc(S2["sq"], 1)
                for q in range(2):
                    act.wait_ge(S2["ss"], q + 1)
                    if q == 0:
                        act.wait_ge(S2["ss"], 1)
                    link(nc.scalar.activation(sq2[:, 8 * q:8 * q + 8, :].rearrange("p t s -> p (t s)"),
                                              pss[:, :, :].rearrange("p t s -> p (t s)"), ACT.Ln, scale=1.0 / P,
                                              bias=eps_col[:, 0:1]))
                    nc.scalar.activation(sq2[:, 8 * q:8 * q + 8, :], sq2[:, 8 * q:8 * q + 8, :], ACT.Exp, scale=-0.5
                                         ).then_inc(S2["rs"], 1)
                act.wait_ge(S2["vt"], 1)
                nc.scalar.activation(v2_rows[:, :, :, :].rearrange("p a h d -> p (a h d)"),
                                     pss[:, :, :].rearrange("p t s -> p (t s)"), ACT.Copy).then_inc(S2["vo"], 1)
                for b in range(2):
                    act.wait_ge(S2["mx"], b + 1)
                    for hh in range(4):
                        nc.scalar.activation(probs2[:, hh, 0:P], pss[:, hh, 0:P], ACT.Exp, bias=negm2[:, 0, hh:hh + 1],
                                             accum_out=den2[:, 0, hh:hh + 1])
                        nc.scalar.activation(probs2[:, hh, P:3 * P], pss[:, hh, P:3 * P], ACT.Exp, bias=negm2[:, 1, hh:hh + 1],
                                             accum_out=den2[:, 1, hh:hh + 1]).then_inc(S2["e"], 1)
                    act.wait_ge(S2["pt"], b + 1)
                    nc.scalar.activation(probs2_t[:, :, :], pss[:, :, 0:3 * P], ACT.Copy).then_inc(S2["pto"], 1)
                    act.wait_ge(S2["pv"], b + 1)
                    nc.scalar.activation(X[:, 4 * b:4 * b + 4, 0:S], pss[:, 0:2, :].rearrange("p t (a s) -> p (t a) s", a=2),
                                         ACT.Copy).then_inc(S2["hi"], 1)
                act.wait_ge(S2["pwm"], 1)
                for t in range(8):
                    ins = nc.scalar.activation(pful[:, t, :], pss[:, t // 2, (t % 2) * S:(t % 2 + 1) * S], ACT.Copy,
                                               scale=P_("pool_scale_2", t, t + 1))
                ins.then_inc(S2["pfu"], 1)
                act.wait_ge(S2["pfu"], 1)
                nc.scalar.activation(X[:, 8:16, 0:S], pful[:, :, :], ACT.Copy).then_inc(S2["phi"], 1)
            if runs("out2"):
                job(J["out2"])
                act.wait_ge(add_done, 16)
                norm_stats(x_res, sq)
                norm_operand(sq)
            if runs("up2a"):
                job(J["up2a"], conv_after(J["up2a"], 0), ACT.Silu)
                job(J["dn2a"])
                job(J["up2b"], conv_after(J["up2b"], 12), ACT.Silu)
                job(J["dn2b"])

        @block.vector
        def _(dve):
            chain = [0]

            def link(ins):
                ins.then_inc(dve_chain, 1)
                chain[0] += 1
                dve.wait_ge(dve_chain, chain[0])

            ln = [0]

            def here(ins):
                ins.then_inc(local, 1)
                ln[0] += 1
                dve.wait_ge(local, ln[0])

            def split(j, i, g, cs):
                for c in cs:
                    s = slot_of(j, g, c)
                    dve.wait_ge(hi_ready, chunk_no(j, i, g, c) - ADA_CHUNKS + 1)
                    nc.vector.tensor_tensor(w_lo[:, s, :, :], raw[:, s, :, :], w_hi[:, s, :, :].bitcast(F32),
                                            ALU.subtract).then_inc(raw_used, 1)

            def take_sum(j, i, g, dst):
                n, b = group_no(j, i, g), bank_of(j, g)
                dve.wait_ge(half_ready, n + 1)
                nc.vector.tensor_tensor(dst, psg[:, b:b + 2, 0:CW], half[:, b // 2, :, :], ALU.add).then_inc(ps_free, 1)

            def job(j, dest, after=None):
                split(j, 0, 0, range(RING, j.chunks[0]))

                def turn(i, last=False):
                    for g in range(len(j.groups)):
                        if g + 1 < len(j.groups):
                            split(j, i, g + 1, range(j.chunks[g + 1]))
                        elif not last:
                            split(j, i + 1, 0, range(j.chunks[0]))
                        elif j.next is not None:
                            split(j.next, 0, 0, range(min(RING, j.next.chunks[0])))
                        take_sum(j, i, g, dest(i, g))
                        if after:
                            after(i, g)
                if j.iters > 1:
                    with dve.Fori(0, j.iters - 1) as i:
                        turn(i)
                turn(j.iters - 1, last=True)

            def bc(ap, shape):
                return ap.broadcast_to(shape)

            nrm = [0]

            def norm_operand(src, fullb, A, B):
                k = nrm[0]
                dve.wait_ge(rs_ready, rsn[0])
                for q in range(4):
                    t = slice(4 * q, 4 * q + 4)
                    here(nc.vector.tensor_tensor(fullb[:, t, :], src[:, t, :], mid(rstd[:, :], 4), ALU.mult))
                    for a in range(4):
                        n = 4 * q + a
                        ins = nc.vector.tensor_scalar(fullb[:, n, :], fullb[:, n, :], A[:, n:n + 1],
                                                      B[:, n:n + 1] if B is not None else None,
                                                      ALU.mult, ALU.add if B is not None else ALU.bypass)
                        if a == 3:
                            ins.then_inc(nrm_full, 1)
                        else:
                            pass
                    dve.wait_ge(nrm_hi, 4 * k + q + 1)
                    nc.vector.tensor_tensor(X[:, t, S:2 * S], fullb[:, t, :], X[:, t, 0:S].bitcast(F32), ALU.subtract
                                            ).then_inc(nrm_out, 1)
                nrm[0] += 1

            rsn = [0]

            def mid(ap, n):
                return ap[:, None, :].broadcast_to((P, n, ap.shape[-1]))

            def last(ap, n):
                return ap[..., None].broadcast_to(tuple(ap.shape) + (n,))

            nc.vector.memset(eps_col[:, 0:1], EPS)
            nc.vector.memset(eps_col[:, 1:2], TINY)
            nc.vector.memset(ones[:, :], 1.0).then_inc(ones_set, 1)
            dve.wait_ge(con_in, 16)
            nc.vector.tensor_copy(ident_bf[:, :], C_("ident"))
            nc.vector.tensor_copy(band_bf[:, :], C_("band_mask")).then_inc(ones_set, 1)

            dve.wait_ge(par_in, 16)

            def ada_turn(i):
                for cb in range(2):
                    if not is_static(i):
                        dve.wait_ge(ada_mm, i * 2 + cb - 1)
                    for k in range(DT):
                        n = cb * DT + k
                        rn = i * 2 * DT + n
                        w = raw[:, n % RING, :, :].rearrange("p k n -> p (k n)")
                        dve.wait_ge(landed[n % RING], 16 * (n // RING + 1) + i * (16 * 2 * DT // RING))
                        acc = ada_acc[:, cb, k % 2, :]
                        ck = P_("c", k, k + 1)
                        if k < 2:
                            nc.vector.tensor_scalar(acc, w, ck, None, ALU.mult).then_inc(raw_used, 1)
                        else:
                            dve.wait_ge(raw_used, rn - 1)
                            nc.vector.scalar_tensor_tensor(acc, w, ck, acc, ALU.mult, ALU.add).then_inc(raw_used, 1)
                    if is_static(i) and cb == 0:
                        continue
                    m = i * 2 + cb - 1
                    dve.wait_ge(ada_mm, m + 1)
                    nc.vector.tensor_tensor(mod[:, ds(m * 8, 8)], pss[:, (cb + 1) % 2, 0:8],
                                            par[:, ds(PAR["b_ada"][0] + m * 8, 8)], ALU.add).then_inc(ada_out, 1)
            turns(dve, 6 * D // ADA_CB // 2, ada_turn)
            dve.wait_ge(ada_mm, 12)
            nc.vector.tensor_tensor(mod[:, 88:96], pss[:, 1, 0:8], P_("b_ada", 88, 96), ALU.add).then_inc(ada_out, 1)
            dve.wait_ge(ada_out, 12)
            M = lambda k: mod[:, k * DT:(k + 1) * DT]
            nc.vector.scalar_tensor_tensor(coef[:, 0, :], M(1), 1.0, P_("g_pre_mix"), ALU.add, ALU.mult)
            nc.vector.scalar_tensor_tensor(coef[:, 1, :], M(4), 1.0, P_("g_pre_ffn"), ALU.add, ALU.mult)
            link(nc.vector.tensor_tensor(coef[:, 2, :], M(2), P_("g_post_mix"), ALU.mult))
            link(nc.vector.tensor_tensor(coef[:, 3, :], M(5), P_("g_post_ffn"), ALU.mult))

            if live:
                split(J["in0"], 0, 0, range(RING))
            rsn[0] += 1
            norm_operand(x1, sq1, coef[:, 0, :], M(0))

            if runs("in"):
                def to_proj(t0):
                    return lambda i, g: proj[:, ds(t0 + 4 * i + 2 * g, 2), :]
                job(J["in0"], to_proj(0))
                job(J["in"], to_proj(2))
                dve.wait_ge(misc_in, 16)
                here(nc.vector.tensor_copy(ang[:, :], pos_i[:, :]))
                here(nc.vector.tensor_scalar(ang[:, :], ang[:, :], C_("inv_freq"), None, ALU.mult))
                here(nc.vector.tensor_scalar(turn[:, :], ang[:, :], 1.0 / (2 * math.pi), 12582912.0, ALU.mult, ALU.add))
                here(nc.vector.tensor_scalar(turn[:, :], turn[:, :], 12582912.0, None, ALU.subtract))
                c1 = 6.28125
                c2 = float(np.float32(np.round((2 * math.pi - c1) * 2 ** 20) / 2 ** 20))
                c3 = 2 * math.pi - c1 - c2
                here(nc.vector.scalar_tensor_tensor(ang[:, :], turn[:, :], -c1, ang[:, :], ALU.mult, ALU.add))
                here(nc.vector.scalar_tensor_tensor(ang[:, :], turn[:, :], -c2, ang[:, :], ALU.mult, ALU.add))
                here(nc.vector.scalar_tensor_tensor(ang[:, :], turn[:, :], -c3, ang[:, :], ALU.mult, ALU.add))
                here(nc.vector.tensor_scalar(red[:, :], ang[:, :], 3.1415925, -3.1415925, ALU.min, ALU.max))
                nc.vector.scalar_tensor_tensor(turn[:, :], red[:, :], -1.0, red[:, :], ALU.mult, ALU.min).then_inc(S1["trig"], 1)
                dve.wait_ge(S1["trig"], 1)
                nc.vector.tensor_scalar(turn[:, :], turn[:, :], math.pi / 2, None, ALU.add).then_inc(S1["trig"], 1)
                dve.wait_ge(S1["tab"], 2)
                nc.vector.tensor_scalar(cosq[:, :], cosk[:, :], HD1 ** -0.5, None, ALU.mult)
                here(nc.vector.tensor_scalar(sinq[:, :], sink_[:, :], HD1 ** -0.5, None, ALU.mult))
                here(nc.vector.tensor_tensor(kr[:, :], proj[:, KA, :], cosk[:, :], ALU.mult))
                dve.wait_ge(S1["swap"], 1)
                here(nc.vector.tensor_tensor(ang[:, :], pss[:, 0, 0:S], sink_[:, :], ALU.mult))
                nc.vector.tensor_tensor(kr[:, :], kr[:, :], ang[:, :], ALU.add).then_inc(S1["kr"], 1)
                here(nc.vector.tensor_tensor(lbc[:, 0, :], P_("lb0"), P_("lb1"), ALU.max))
                nc.vector.tensor_tensor(lbc[:, 1, :], P_("lb0"), lbc[:, 0, :], ALU.subtract)
                nc.vector.tensor_tensor(lbc[:, 2, :], P_("lb1"), lbc[:, 0, :], ALU.subtract).then_inc(SH["lbm"], 1)
                dve.wait_ge(SH["lbe"], 1)
                here(nc.vector.tensor_tensor(lbc[:, 3, :], lbc[:, 1, :], lbc[:, 2, :], ALU.add))
                here(nc.vector.reciprocal(lbc[:, 3, :], lbc[:, 3, :]))
                here(nc.vector.tensor_tensor(lbc[:, 4, :], lbc[:, 1, :], lbc[:, 3, :], ALU.mult))
                here(nc.vector.tensor_scalar(lbc[:, 5, :], lbc[:, 4, :], -1.0, 1.0, ALU.mult, ALU.add))
                dve.wait_ge(SH["act"], 3)
                for h in range(HGH):
                    ins = nc.vector.tensor_scalar(proj[:, FH + h, :], proj[:, FH + h, :], lbc[:, 5, h:h + 1],
                                                  lbc[:, 4, h:h + 1], ALU.mult, ALU.add)
                ins.then_inc(SH["prep"], 1)
                for b in range(4):
                    dve.wait_ge(S1["qswap"], b + 1)
                    nc.vector.tensor_tensor(q_cos[:, :, :], proj[:, QA + 2 * b:QA + 2 * b + 2, :], mid(cosq[:, :], 2), ALU.mult)
                    here(nc.vector.tensor_tensor(q_sin[:, :, :], pss[:, 0, :].rearrange("p (a s) -> p a s", a=2),
                                                 mid(sinq[:, :], 2), ALU.mult))
                    nc.vector.tensor_tensor(qr[:, :, :], q_cos[:, :, :], q_sin[:, :, :], ALU.add).then_inc(S1["qr"], 1)
                    dve.wait_ge(S1["s"], b + 1)
                    nc.vector.tensor_reduce(mx[:, 0, :], pss[:, :, 0:P], AX.X, ALU.max)
                    here(nc.vector.tensor_reduce(mx[:, 1, :], pss[:, :, P:3 * P], AX.X, ALU.max))
                    sk = P_("sinks", 4 * b, 4 * b + 4)
                    here(nc.vector.tensor_tensor(mx1[:, :, :], mx[:, :, :], mid(sk, 2), ALU.max))
                    here(nc.vector.tensor_scalar(negm[:, :, :], mx1[:, :, :], -1.0, None, ALU.mult))
                    nc.vector.tensor_tensor(es[:, :, :], negm[:, :, :], mid(sk, 2), ALU.add).then_inc(S1["mx"], 1)
                    dve.wait_ge(S1["es"], b + 1)
                    here(nc.vector.tensor_tensor(den[:, :, :], den[:, :, :], es[:, :, :], ALU.add))
                    here(nc.vector.reciprocal(den[:, :, :], den[:, :, :]))
                    nc.vector.tensor_tensor(probs[:, :, 0:P], probs[:, :, 0:P], last(den[:, 0, :], P), ALU.mult)
                    nc.vector.tensor_tensor(probs[:, :, P:3 * P], probs[:, :, P:3 * P], last(den[:, 1, :], 2 * P), ALU.mult
                                            ).then_inc(S1["pn"], 1)
                    dve.wait_ge(S1["hi"], b + 1)
                    nc.vector.tensor_tensor(attn_x[:, 2 * b:2 * b + 2, S:2 * S], pss[:, 0, :].rearrange("p (a s) -> p a s", a=2),
                                            attn_x[:, 2 * b:2 * b + 2, 0:S].bitcast(F32), ALU.subtract).then_inc(S1["lo"], 1)

                cum = decay[:, 6, :]
                PER = 4

                def head(h):
                    f = proj[:, ds(FH + h, 1), :].rearrange("p a s -> p (a s)")
                    k = [0]

                    def step(ins):
                        ins.then_inc(hl, 1)
                        k[0] += 1
                        dve.wait_ge(hl, h * PER + k[0])
                    if not is_static(h):
                        dve.wait_ge(SH["o"], h)
                    nc.vector.tensor_scalar(hg_k[:, :], f, -1.0, 1.0, ALU.mult, ALU.add)
                    dve.wait_ge(SH["ln"], h + 1)
                    step(nc.vector.tensor_tensor_scan(cum, C_("chunk_scan"), hg_l[:, :], 0.0, ALU.mult, ALU.add))
                    for n, m in enumerate(LEVELS):
                        b4 = cum.rearrange("p (n t m) -> p n t m", t=2, m=m)
                        d4 = decay[:, n, :].rearrange("p (n t m) -> p n t m", t=2, m=m)
                        ref = b4[:, :, 0, m - 1:m].broadcast_to((P, S // (2 * m), m))
                        nc.vector.tensor_tensor(d4[:, :, 1, :], b4[:, :, 1, :], ref, ALU.subtract)
                        nc.vector.tensor_tensor(d4[:, :, 0, :], ref, b4[:, :, 0, :], ALU.subtract)
                    c3_ = cum.rearrange("p (n m) -> p n m", m=CH)
                    nc.vector.tensor_tensor(decay[:, 7, :].rearrange("p (n m) -> p n m", m=CH),
                                            c3_[:, :, CH - 1:CH].broadcast_to((P, S // CH, CH)), c3_,
                                            ALU.subtract).then_inc(SH["d"], 1)
                    dve.wait_ge(SH["exp"], h + 1)
                    dve.wait_ge(SH["cp"], 2 * h + 2)
                    nc.vector.tensor_tensor(Pq[:, :, :], decay[:, 0:7, :], mid(hg_q[:, :], 7), ALU.mult)
                    nc.vector.tensor_tensor(Rk[:, 0:6, :], decay[:, 0:6, :], mid(hg_k[:, :], 6), ALU.mult)
                    step(nc.vector.tensor_tensor(Rk[:, 6, :], decay[:, 7, :], hg_k[:, :], ALU.mult))
                    nc.vector.tensor_copy(p_c[:, 0:CH], Pq[:, 6, 2 * CH:3 * CH])
                    nc.vector.tensor_scalar(p_c[:, CH:2 * CH], Pq[:, 6, 3 * CH:4 * CH], decay[:, 6, 3 * CH - 1:3 * CH], None, ALU.mult)
                    nc.vector.tensor_scalar(r_c[:, 0:CH], Rk[:, 6, 0:CH], decay[:, 6, 2 * CH - 1:2 * CH], None, ALU.mult)
                    nc.vector.tensor_copy(r_c[:, CH:2 * CH], Rk[:, 6, CH:2 * CH]).then_inc(SH["pr"], 1)
                    dve.wait_ge(SH["pr"], h + 1)
                    for a, (s_, m_) in enumerate((("sa", "ma"), ("sb", "mb"))):
                        dve.wait_ge(SH[s_], h + 1)
                        step(nc.vector.tensor_tensor(masked[:, :, :].rearrange("p l s -> p (l s)"),
                                                     pss[:, 2 * a:2 * a + 2, :].rearrange("p t s -> p (t s)"),
                                                     C_("level_mask"), ALU.mult))
                        nc.vector.tensor_reduce(s_ab[:, a, :], masked[:, :, :].rearrange("p l s -> p s l"), AX.X, ALU.add
                                                ).then_inc(SH[m_], 1)
                        dve.wait_ge(SH[m_], h + 1)
                    assert k[0] == PER, k
                turns(dve, HGH, head)
                dve.wait_ge(SH["rs"], 1)
                o_all = proj[:, IH:IH + 8, :]
                here(nc.vector.scalar_tensor_tensor(flat(hfull), flat3(o_all), P_("hg_norm"), flat(hrs), ALU.mult, ALU.mult))
                nc.vector.tensor_tensor(hfull[:, :, :], hfull[:, :, :], proj[:, GH:GH + 8, :], ALU.mult).then_inc(SH["full"], 1)
                dve.wait_ge(SH["hi"], 1)
                nc.vector.tensor_tensor(hgrn_x[:, :, S:2 * S], hfull[:, :, :], hgrn_x[:, :, 0:S].bitcast(F32), ALU.subtract
                                        ).then_inc(SH["lo"], 1)

            if runs("merge"):
                j = J["merge"]

                def after(i, g):
                    n = group_no(j, i, g)
                    if g == 1:
                        dve.wait_ge(gate_ready, 2 * i + 1)
                        dve.wait_ge(ps_free, n + 1)
                        nc.vector.tensor_tensor(u_a[:, :, :], u_a[:, :, :], sg_a[:, :, :], ALU.mult)
                    if g == 3:
                        dve.wait_ge(gate_ready, 2 * i + 2)
                        dve.wait_ge(ps_free, n + 1)
                        nc.vector.tensor_tensor(u_h[:, :, :], u_h[:, :, :], sg_h[:, :, :], ALU.mult).then_inc(mul_done, 1)
                        dve.wait_ge(mul_done, i + 1)
                        nc.vector.tensor_tensor(full[:, :, :], u_a[:, :, :], u_h[:, :, :], ALU.add).then_inc(full_ready, 1)
                        dve.wait_ge(fhi_ready, i + 1)
                        nc.vector.tensor_tensor(merged[:, ds(2 * i, 2), S:2 * S], full[:, :, :],
                                                merged[:, ds(2 * i, 2), 0:S].bitcast(F32), ALU.subtract).then_inc(opnd_ready, 1)
                job(j, lambda i, g: (t_a, u_a, t_h, u_h)[g][:, :, :], after)

            def residual(dst, coefs, k, first):
                rsn[0] += 1
                dve.wait_ge(rs_ready, rsn[0])
                for q in range(4):
                    t = slice(4 * q, 4 * q + 4)
                    here(nc.vector.tensor_tensor(y[:, t, :], y[:, t, :], mid(rstd[:, :], 4), ALU.mult))
                    for a in range(4):
                        n = 4 * q + a
                        ins = nc.vector.scalar_tensor_tensor(x_res[:, n, :], y[:, n, :], coefs[:, n:n + 1], x_res[:, n, :],
                                                             ALU.mult, ALU.add)
                ins.then_inc(y_ready, 1)
                dve.wait_ge(y_ready, k)

            def to_y(step, per):
                return lambda i, g: y[:, ds(step * i + 2 * g, 2), :]

            if runs("out"):
                job(J["out"], to_y(4, 2))
                dve.wait_ge(x_back, 16)
                residual(x_res, coef[:, 2, :], 1, True)
                rsn[0] += 1
                norm_operand(x_res, sq, coef[:, 1, :], M(3))

            def swiglu(j, k0, g0):
                def after(i, g):
                    if g == 1:
                        dve.wait_ge(gate_ready, g0 + i + 1)
                        dve.wait_ge(ps_free, group_no(j, i, g) + 1)
                        nc.vector.tensor_tensor(fullf[:, :, :], t_u[:, :, :], sg[:, :, :], ALU.mult).then_inc(full_ready, 1)
                        dve.wait_ge(fhi_ready, k0 + i + 1)
                        nc.vector.tensor_tensor(hid[:, ds(2 * i, 2), S:2 * S], fullf[:, :, :],
                                                hid[:, ds(2 * i, 2), 0:S].bitcast(F32), ALU.subtract).then_inc(opnd_ready, 1)
                return after

            def add_y(j, dst):
                def after(i, g):
                    dve.wait_ge(ps_free, group_no(j, i, g) + 1)
                    d = dst[:, ds(2 * (len(j.groups) * i + g), 2), :]
                    nc.vector.tensor_tensor(d, d, t_g2[:, :, :], ALU.add).then_inc(add_done, 1)
                    dve.wait_ge(add_done, addn[j.name] + i * len(j.groups) + g + 1)
                return after
            t_g2 = t_g
            addn = {"dn1b": 0, "out2": 8, "dn2b": 16}

            if runs("up1a"):
                job(J["up1a"], lambda i, g: (t_g, t_u)[g][:, :, :], swiglu(J["up1a"], 8, 16))
                job(J["dn1a"], to_y(4, 2))
                job(J["up1b"], lambda i, g: (t_g, t_u)[g][:, :, :], swiglu(J["up1b"], 20, 28))
                job(J["dn1b"], lambda i, g: t_g[:, :, :], add_y(J["dn1b"], y))
                residual(x_res, coef[:, 3, :], 2, False)
                rsn[0] += 1
                norm_operand(x_res, sq, P_("attn_norm_g_2"), None)

            if runs("in2"):
                job(J["in2"], lambda i, g: proj2[:, ds(4 * i + 2 * g, 2), :])
                dve.wait_ge(S2["row"], 1)
                nc.vector.memset(bias_row[0:HEADS2, S:], NEG).then_inc(S2["rowo"], 1)
                nc.vector.tensor_copy(bias_row[0:HEADS2, 0:S], pss[0:HEADS2, 0, 0:S]).then_inc(S2["rowo"], 1)
                here(nc.vector.tensor_scalar(den2[:, 0, 0:1], P_("q_norm_g_2"), P ** -0.5, None, ALU.mult))
                dve.wait_ge(S2["rs"], 2)
                q8, k8 = proj2[:, Q2:Q2 + 8, :], proj2[:, K2:K2 + 8, :]
                nc.vector.scalar_tensor_tensor(flat3(q8), flat3(q8), den2[:, 0, 0:1], flat3(sq2[:, 0:8, :]), ALU.mult, ALU.mult)
                nc.vector.scalar_tensor_tensor(flat3(k8), flat3(k8), P_("k_norm_g_2"), flat3(sq2[:, 8:16, :]), ALU.mult, ALU.mult
                                               ).then_inc(S2["qk"], 1)
                dve.wait_ge(S2["qk"], 1)
                for b in range(2):
                    dve.wait_ge(S2["s"], b + 1)
                    nc.vector.tensor_reduce(mx2[:, 0, :], pss[:, :, 0:P], AX.X, ALU.max)
                    here(nc.vector.tensor_reduce(mx2[:, 1, :], pss[:, :, P:3 * P], AX.X, ALU.max))
                    nc.vector.tensor_scalar(negm2[:, :, :], mx2[:, :, :], -1.0, None, ALU.mult).then_inc(S2["mx"], 1)
                    dve.wait_ge(S2["e"], 4 * b + 4)
                    here(nc.vector.reciprocal(den2[:, :, :], den2[:, :, :]))
                    nc.vector.tensor_tensor(probs2[:, :, 0:P], probs2[:, :, 0:P], last(den2[:, 0, :], P), ALU.mult)
                    nc.vector.tensor_tensor(probs2[:, :, P:3 * P], probs2[:, :, P:3 * P], last(den2[:, 1, :], 2 * P), ALU.mult
                                            ).then_inc(S2["pn"], 1)
                    dve.wait_ge(S2["hi"], b + 1)
                    nc.vector.tensor_tensor(X[:, 4 * b:4 * b + 4, S:2 * S], pss[:, 0:2, :].rearrange("p t (a s) -> p (t a) s", a=2),
                                            X[:, 4 * b:4 * b + 4, 0:S].bitcast(F32), ALU.subtract).then_inc(S2["lo"], 1)
                p8 = proj2[:, P2:P2 + 8, :]
                nc.vector.memset(pa[:, :, 0:16], 0.0)
                nc.vector.memset(pb_[:, :, 0:16], 0.0)
                nc.vector.memset(pc[:, :, 0:16], 0.0)
                here(nc.vector.tensor_copy(pa[:, :, 16:], p8))
                here(nc.vector.tensor_tensor(pb_[:, :, 1:], pa[:, :, 1:], pa[:, :, :PW - 1], ALU.add))
                here(nc.vector.tensor_tensor(pc[:, 2:, 3:], pb_[:, 2:, 3:], pb_[:, 2:, 1:PW - 2], ALU.add))
                here(nc.vector.tensor_tensor(pb_[:, 4:, 7:], pc[:, 4:, 7:], pc[:, 4:, 3:PW - 4], ALU.add))
                here(nc.vector.tensor_tensor(pc[:, 6:, 15:], pb_[:, 6:, 15:], pb_[:, 6:, 7:PW - 8], ALU.add))
                for g in range(4):
                    t = slice(2 * g, 2 * g + 2)
                    src = (pb_, pc)[g % 2]
                    cnt = C_("inv_count", g * S, (g + 1) * S)
                    here(nc.vector.tensor_tensor(pmix[:, t, :], src[:, t, 16:], mid(cnt, 2), ALU.mult))
                    ins = nc.vector.tensor_tensor(pmix[:, t, :], pmix[:, t, :], p8[:, t, :], ALU.subtract)
                ins.then_inc(S2["mix"], 1)
                dve.wait_ge(S2["phi"], 1)
                nc.vector.tensor_tensor(X[:, 8:16, S:2 * S], pful[:, :, :], X[:, 8:16, 0:S].bitcast(F32), ALU.subtract
                                        ).then_inc(S2["plo"], 1)
            if runs("out2"):
                job(J["out2"], lambda i, g: t_g[:, :, :], add_y(J["out2"], x_res))
                rsn[0] += 1
                norm_operand(x_res, sq, P_("ffn_norm_g_2"), None)

            def conv(j, k0, f0, g0):
                def after(i, g):
                    t0 = (24 if j.name == "up2b" else 0) + (HIDT if g else 0)
                    n = 4 * (k0 + i) + 2 * g
                    for tap_ in (1, 0):
                        for a in range(2):
                            if tap_ == 1:
                                dve.wait_ge(SC["aff"], n + a + 1)
                            o = PAR["conv_w_2"][0] + tap_ * 2 * HIDT + t0 + a
                            ins = nc.vector.scalar_tensor_tensor(cacc[:, g, a, :], cu[:, g, a, tap_:tap_ + CW],
                                                                 par[:, ds(2 * i + o, 1)], cacc[:, g, a, :],
                                                                 ALU.mult, ALU.add)
                            if a == 1 and tap_ == 1:
                                ins.then_inc(cmid, 1)
                                dve.wait_ge(cmid, 2 * (k0 + i) + g + 1)
                    ins.then_inc(SC["acc"], 1)
                    if g == 1:
                        dve.wait_ge(gate_ready, g0 + i + 1)
                        dve.wait_ge(SC["acc"], 2 * (k0 + i) + 2)
                        nc.vector.tensor_tensor(cful[:, :, :], cacc[:, 1, :, :], csg[:, :, :], ALU.mult).then_inc(full_ready, 1)
                        dve.wait_ge(fhi_ready, f0 + i + 1)
                        nc.vector.tensor_tensor(hid[:, ds(2 * i, 2), S:2 * S], cful[:, :, :],
                                                hid[:, ds(2 * i, 2), 0:S].bitcast(F32), ALU.subtract).then_inc(opnd_ready, 1)
                return after
            if runs("up2a"):
                here(nc.vector.memset(cu[:, :, :, 0:2], 0.0))
                job(J["up2a"], lambda i, g: cu[:, g, :, 2:], conv(J["up2a"], 0, 30, 38))
                job(J["dn2a"], to_y(4, 2))
                here(nc.vector.memset(cu[:, :, :, 0:2], 0.0))
                job(J["up2b"], lambda i, g: cu[:, g, :, 2:], conv(J["up2b"], 12, 42, 50))
                job(J["dn2b"], lambda i, g: t_g[:, :, :], add_y(J["dn2b"], y))
                for q in range(4):
                    t = slice(4 * q, 4 * q + 4)
                    nc.vector.tensor_tensor(x_res[:, t, :], x_res[:, t, :], y[:, t, :], ALU.add).then_inc(y_ready, 1)

        @block.tensor
        def _(pe):
            def mm(out_, l, r_, start=True, stop=True):
                return nc.tensor.matmul(out_, l, r_, start=start, stop=stop)

            def job(j, xs, ready=None):
                def turn(i):
                    for g in range(len(j.groups)):
                        n, b = group_no(j, i, g), bank_of(j, g)
                        kt = j.groups[g][2]
                        if not (is_static(i) and n < 2):
                            pe.wait_ge(ps_free, n - 1)
                        for c in range(j.chunks[g]):
                            s = slot_of(j, g, c)
                            if ready and is_static(i) and i == 0:
                                ready(g, c)
                            pe.wait_ge(raw_used, chunk_no(j, i, g, c) + 1)
                            for k in range(KC):
                                kk = c * KC + k
                                x = xs(g)
                                for t in range(2):
                                    hi = w_hi[:, s, k, t * P:(t + 1) * P]
                                    lo = w_lo[:, s, k, t * P:(t + 1) * P]
                                    o = psg[:, b + t, :]
                                    first, final = kk == 0, kk == kt - 1
                                    if not final:
                                        mm(o, hi, x[:, kk, :], first, False)
                                        ins = mm(o[:, 0:S], lo, x[:, kk, 0:S], False, False)
                                    else:
                                        mm(o[:, 0:S], lo, x[:, kk, 0:S], False, False)
                                        ins = mm(o, hi, x[:, kk, :], False, True)
                            ins.then_inc(pe_chunk, 1)
                turns(pe, j.iters, turn)

            nrm = [0]

            def norm_sum(sqb):
                pe.wait_ge(ones_set, 1)
                for q in range(4):
                    pe.wait_ge(sq_ready, 4 * nrm[0] + q + 1)
                    for a in range(4):
                        t = 4 * q + a
                        ins = mm(pss[:, 0, 0:S], ones[:, :], sqb[:, t, :], t == 0, t == DT - 1)
                ins.then_inc(ss_ready, 1)
                nrm[0] += 1

            nop = [0]

            def x_ready():
                k = nop[0]
                nop[0] += 1

                def ready(g, c):
                    if g == 0 and c < 4:
                        pe.wait_ge(nrm_out, 4 * k + c + 1)
                return ready

            norm_sum(sq1)

            def ada_turn(i):
                for cb in range(2):
                    m = i * 2 + cb
                    pe.wait_ge(raw_used, (m + 1) * DT)
                    if not is_static(i):
                        pe.wait_ge(ada_out, m - 1)
                    elif cb == 0:
                        pe.wait_ge(rs_ready, 1)
                    for t in range(8):
                        for a in range(2):
                            ins = mm(pss[:, cb, t:t + 1], ada_acc[:, cb, a, t * P:(t + 1) * P], ones[:, 0:1], a == 0, a == 1)
                    ins.then_inc(ada_mm, 1)
            turns(pe, 6 * D // ADA_CB // 2, ada_turn)
            if runs("in"):
                job(J["in0"], lambda g: X, x_ready())
                job(J["in"], lambda g: X)
                pe.wait_ge(con_in, 16)
                pe.wait_ge(ones_set, 2)
                pe.wait_ge(ps_free, J["merge"].G0)
                mm(pss[:, 0, 0:S], C_("rope_swap"), proj[:, KA, :]).then_inc(S1["swap"], 1)
                for a in range(2):
                    ins = nc.tensor.transpose(pss[:, 2, a * P:(a + 1) * P], proj[:, VA, a * P:(a + 1) * P], C_("ident"))
                ins.then_inc(S1["vt"], 1)
                pe.wait_ge(S1["kr"], 1)
                for g in range(2):
                    mm(pss[:, 1, g * S:(g + 1) * S], C_("kv_pick", g * P, (g + 1) * P), kr[:, :]).then_inc(S1["dup"], 1)
                pe.wait_ge(S1["dupo"], 1)
                pe.wait_ge(S1["vo"], 1)
                for b in range(4):
                    g = b // 2
                    if b:
                        pe.wait_ge(S1["lo"], b)
                    mm(pss[:, 0, :], C_("rope_swap"), proj[:, QA + 2 * b:QA + 2 * b + 2, :].rearrange("p a s -> p (a s)")
                       ).then_inc(S1["qswap"], 1)
                    pe.wait_ge(S1["qr"], b + 1)
                    for hh in range(4):
                        rows = slice(HD1 * (hh % 2), HD1 * (hh % 2) + HD1)
                        for a, (lo_, hi_) in enumerate(((0, P), (P, 3 * P))):
                            o = pss[:, hh, lo_:hi_]
                            mm(o, ident_bf[:, :], band_bf[:, lo_:hi_], True, False)
                            ins = mm(o, qr[rows, hh // 2, a * P:(a + 1) * P], kdup[rows, g, 0:hi_ - lo_], False, True)
                    ins.then_inc(S1["s"], 1)
                    pe.wait_ge(S1["pn"], b + 1)
                    for hh in range(4):
                        for a in range(3):
                            ins = nc.tensor.transpose(pss[:, hh, a * P:(a + 1) * P], probs[:, hh, a * P:(a + 1) * P], C_("ident"))
                    ins.then_inc(S1["pt"], 1)
                    pe.wait_ge(S1["pto"], b + 1)
                    for hh in range(4):
                        r0 = HD1 * (hh % 2)
                        o = pss[r0:r0 + HD1, 0, (hh // 2) * S:(hh // 2 + 1) * S]
                        v0, v1 = (v_sb[:, a, HD1 * g:HD1 * (g + 1)] for a in range(2))
                        mm(o[:, 0:P], v0, probs_t[:, hh, 0:P])
                        mm(o[:, P:S], v0, probs_t[:, hh, P:2 * P], True, False)
                        ins = mm(o[:, P:S], v1, probs_t[:, hh, 2 * P:3 * P], False, True)
                    ins.then_inc(S1["pv"], 1)
                pe.wait_ge(S1["lo"], 4)

                def head(h):
                    pe.wait_ge(SH["cp"], 2 * h + 2)
                    if not is_static(h):
                        pe.wait_ge(SH["oo"], h)
                    for a in range(2):
                        ins = nc.tensor.transpose(pss[:, 0, a * P:(a + 1) * P], hg_v[:, a * P:(a + 1) * P], C_("ident"))
                    ins.then_inc(SH["vt"], 1)
                    pe.wait_ge(SH["vo"], h + 1)
                    pe.wait_ge(SH["pr"], h + 1)
                    for a, s_ in enumerate(("sa", "sb")):
                        c = slice(a * P, (a + 1) * P)
                        for n in range(8):
                            l, r_ = (Rk[:, n, c], Pq[:, n, c]) if n < 7 else (hg_k[:, c], hg_q[:, c])
                            ins = mm(pss[:, 2 * a + n // 4, (n % 4) * P:(n % 4 + 1) * P], l, r_)
                        ins.then_inc(SH[s_], 1)
                    pe.wait_ge(SH["ma"], h + 1)
                    mm(pss[:, 0, 0:P], r_c[:, :], p_c[:, :]).then_inc(SH["sc"], 1)
                    pe.wait_ge(SH["sco"], h + 1)
                    pe.wait_ge(SH["mb"], h + 1)
                    mm(pss[:, 2, 0:P], v_rows[:, 0, :], s_ab[:, 0, :])
                    mm(pss[:, 2, P:S], v_rows[:, 0, :], s_c[:, :], True, False)
                    mm(pss[:, 2, P:S], v_rows[:, 1, :], s_ab[:, 1, :], False, True).then_inc(SH["o"], 1)
                turns(pe, HGH, head)
                pe.wait_ge(SH["sq"], 1)
                for n in range(4):
                    ins = mm(pss[:, n, :], ones[:, :], hsq[:, 2 * n:2 * n + 2, :].rearrange("p a s -> p (a s)"))
                ins.then_inc(SH["ss"], 1)
            if runs("merge"):
                def ready(g, c):
                    if (g, c) == (1, 0):
                        pe.wait_ge(S1["lo"], 4)
                    if (g, c) == (3, 0):
                        pe.wait_ge(SH["lo"], 1)
                job(J["merge"], lambda g: (X, attn_x, X, hgrn_x)[g], ready)

            def operand_ready(k0):
                def ready(g, c):
                    if g == 0:
                        pe.wait_ge(opnd_ready, k0 + 2 * c + 2)
                return ready
            if runs("out"):
                job(J["out"], lambda g: merged, operand_ready(0))
                norm_sum(sq)
                pe.wait_ge(rs_ready, nrm[0])
                norm_sum(sq)
            if runs("up1a"):
                job(J["up1a"], lambda g: X, x_ready())
                job(J["dn1a"], lambda g: hid, operand_ready(8))
                job(J["up1b"], lambda g: X)
                job(J["dn1b"], lambda g: hid, operand_ready(20))
                norm_sum(sq)
                pe.wait_ge(rs_ready, nrm[0])
                norm_sum(sq)
            if runs("in2"):
                job(J["in2"], lambda g: X, x_ready())
                pe.wait_ge(misc_in, 48)
                mm(pss[0:HEADS2, 0, 0:S], relb[0:BUCKETS, :], hot[0:BUCKETS, :]).then_inc(S2["row"], 1)
                pe.wait_ge(S2["rowo"], 2)
                for q in range(2):
                    pe.wait_ge(S2["sq"], 2 * q + 2)
                    if q:
                        pe.wait_ge(S2["rs"], 1)
                    for n in range(4):
                        t = 8 * q + 2 * n
                        ins = mm(pss[:, n, :], ones[:, :], sq2[:, t:t + 2, :].rearrange("p a s -> p (a s)"))
                    ins.then_inc(S2["ss"], 1)
                pe.wait_ge(S2["rs"], 2)
                for a in range(2):
                    for h in range(8):
                        n = a * 8 + h
                        ins = nc.tensor.transpose(pss[:, n // 4, (n % 4) * P:(n % 4 + 1) * P],
                                                  proj2[:, V2 + h, a * P:(a + 1) * P], C_("ident"))
                ins.then_inc(S2["vt"], 1)
                pe.wait_ge(S2["vo"], 1)
                pe.wait_ge(S2["qk"], 1)
                pe.wait_ge(S2["hk"], 16)
                for b in range(2):
                    if b:
                        pe.wait_ge(S2["lo"], b)
                    for hh in range(4):
                        h = 4 * b + hh
                        for a, (lo_, hi_) in enumerate(((0, P), (P, 3 * P))):
                            o = pss[:, hh, lo_:hi_]
                            mm(o, C_("flip"), hank[:, h, P * (1 - a):S], True, False)
                            ins = mm(o, proj2[:, Q2 + h, a * P:(a + 1) * P], proj2[:, K2 + h, 0:hi_ - lo_], False, True)
                    ins.then_inc(S2["s"], 1)
                    pe.wait_ge(S2["pn"], b + 1)
                    for hh in range(4):
                        for a in range(3):
                            ins = nc.tensor.transpose(pss[:, hh, a * P:(a + 1) * P], probs2[:, hh, a * P:(a + 1) * P], C_("ident"))
                    ins.then_inc(S2["pt"], 1)
                    pe.wait_ge(S2["pto"], b + 1)
                    for hh in range(4):
                        h = 4 * b + hh
                        o = pss[:, hh // 2, (hh % 2) * S:(hh % 2 + 1) * S]
                        v0, v1 = (v2_rows[:, a, h, :] for a in range(2))
                        mm(o[:, 0:P], v0, probs2_t[:, hh, 0:P])
                        mm(o[:, P:S], v0, probs2_t[:, hh, P:2 * P], True, False)
                        ins = mm(o[:, P:S], v1, probs2_t[:, hh, 2 * P:3 * P], False, True)
                    ins.then_inc(S2["pv"], 1)
                pe.wait_ge(S2["lo"], 2)
                pe.wait_ge(S2["mix"], 1)
                pe.wait_ge(S2["pw"], 16)
                for g in range(4):
                    for n in range(2):
                        for k in range(2):
                            ins = mm(pss[:, g, n * S:(n + 1) * S], pwt[:, g, k, n * P:(n + 1) * P], pmix[:, 2 * g + k, :], k == 0, k == 1)
                ins.then_inc(S2["pwm"], 1)
            if runs("out2"):
                def ready(g, c):
                    if (g, c) == (0, 0):
                        pe.wait_ge(S2["lo"], 2)
                    if (g, c) == (0, 2):
                        pe.wait_ge(S2["plo"], 1)
                job(J["out2"], lambda g: X, ready)
                norm_sum(sq)
            if runs("up2a"):
                job(J["up2a"], lambda g: X, x_ready())
                job(J["dn2a"], lambda g: hid, operand_ready(30))
                job(J["up2b"], lambda g: X)
                job(J["dn2b"], lambda g: hid, operand_ready(42))


def kernel(**inputs):
    import concourse.bacc as _bacc
    from concourse import mybir as _mybir
    from concourse.bass_utils import run_bass_kernel_spmd as _run

    f = {k: np.asarray(v) for k, v in inputs.items()}

    def cols(a, t):
        return np.ascontiguousarray(a.reshape(t, P).T)

    packed = {
        "c": cols(f["c"][0], DT), "b_ada": cols(f["b_ada"][0], 6 * DT), "g_pre_mix": cols(f["g_pre_mix"][0], DT),
        "g_post_mix": cols(f["g_post_mix"][0], DT), "g_pre_ffn": cols(f["g_pre_ffn"][0], DT),
        "g_post_ffn": cols(f["g_post_ffn"][0], DT), "sinks": np.broadcast_to(f["attn_sinks"][0], (P, HEADS1)),
        "lb0": cols(f["hg_lower_bounds"][0], HGH), "lb1": cols(f["hg_lower_bounds"][1], HGH),
        "hg_norm": cols(f["hg_norm"][0], 1), "attn_norm_g_2": cols(f["attn_norm_g_2"][0], DT),
        "q_norm_g_2": cols(f["q_norm_g_2"][0], 1), "k_norm_g_2": cols(f["k_norm_g_2"][0], 1),
        "pool_scale_2": cols(f["pool_scale_2"][0], 8), "ffn_norm_g_2": cols(f["ffn_norm_g_2"][0], DT),
        "conv_w_2": cols(f["conv_w_2"][0], 3 * 2 * HIDT), "conv_b_2": cols(f["conv_b_2"][0], 2 * HIDT),
    }
    con, hot = constants()
    arrays = {
        "xT": np.ascontiguousarray(f["x"][0].T), "params": np.concatenate([packed[n] for n in PAR], axis=1),
        "cons": con, "hot_in": hot, "rel_bias": np.ascontiguousarray(f["rel_bias_2"].T), "pos": f["positions"][0],
        "w_ada": f["w_ada"][0], "w_in": f["w_in"][0], "w_attn": f["w_attn_proj"][0], "w_hgrn": f["w_hgrn_proj"][0],
        "w_out": f["w_out"][0], "w_ffn_in": f["w_ffn_in"][0], "w_ffn_out": f["w_ffn_out"][0], "w_in2": f["w_in_2"][0],
        "pool_w": f["pool_w_2"][0], "w_out2": f["w_out_2"][0], "w_up": f["w_up_2"][0], "w_down": f["w_down_2"][0],
    }
    nc = _bacc.Bacc("TRN2", target_bir_lowering=False, num_devices=1)
    args = {}
    ins = {}
    for name, a in arrays.items():
        a = np.ascontiguousarray(a)
        ins[f"in_{name}"] = a
        args[name] = nc.dram_tensor(f"in_{name}", a.shape, _mybir.dt.from_np(a.dtype), kind="ExternalInput").ap()
    out = nc.dram_tensor("out_T", (D, S), _mybir.dt.float32, kind="ExternalOutput").ap()
    two_block_kernel(nc, out=out, **args)
    r = _run(nc, [ins], core_ids=[0])
    return np.ascontiguousarray(r.results[0]["out_T"].T)[None]
```

```python
import math
import numpy as np
import concourse.bass as bass
from concourse import mybir
from contextlib import ExitStack

F32 = mybir.dt.float32
R32 = mybir.dt.float32r
BF16 = mybir.dt.bfloat16
I32 = mybir.dt.int32
ALU = mybir.AluOpType
ACT = mybir.ActivationFunctionType
AX = mybir.AxisListType
ds = bass.ds

P = 128
S = 256
D = 2048
DT = D // P
HEADS1, KV1, HD1 = 16, 2, 64
ROT = HD1 // 4
THETA = 500000.0
HGH = 8
CH = 64
LEVELS = (32, 16, 8, 4, 2, 1)
HID = 5632
HIDT = HID // P
HEADS2 = 8
BUCKETS, MAX_DIST = 32, 1024
WINDOWS = (2, 4, 8, 16)
EPS = 1e-6
NEG = -1e30
TINY = 1e-19

KC = 4
CW = 256
RING = 4
ADA_CB = 1024

PAR = {}
_n = 0
for _name, _w in (("c", DT), ("b_ada", 6 * DT), ("g_pre_mix", DT), ("g_post_mix", DT), ("g_pre_ffn", DT),
                  ("g_post_ffn", DT), ("sinks", HEADS1), ("lb0", HGH), ("lb1", HGH), ("hg_norm", 1),
                  ("attn_norm_g_2", DT), ("q_norm_g_2", 1), ("k_norm_g_2", 1), ("pool_scale_2", 8),
                  ("ffn_norm_g_2", DT), ("conv_w_2", 3 * 2 * HIDT), ("conv_b_2", 2 * HIDT)):
    PAR[_name] = (_n, _n + _w)
    _n += _w
NPAR = _n

CON = {}
_n = 0
for _name, _w in (("ident", P), ("flip", P), ("rope_swap", P), ("kv_pick", 2 * P),
                  ("inv_freq", 1), ("band_mask", 3 * P), ("chunk_scan", S)):
    CON[_name] = (_n, _n + _w)
    _n += _w
NCON = _n
HANKEL_W = 3 * P


def constants():
    con = np.zeros((P, NCON), np.float32)
    p = np.arange(P)

    def put(name, a):
        con[:, CON[name][0]:CON[name][1]] = a.reshape(P, -1)

    put("ident", np.eye(P))
    put("flip", np.eye(P)[::-1])
    swap = np.zeros((P, P))
    half = ROT // 2
    for head in range(P // HD1):
        for d in range(half):
            swap[head * HD1 + d + half, head * HD1 + d] = -1.0
            swap[head * HD1 + d, head * HD1 + d + half] = 1.0
    put("rope_swap", swap)
    pick = np.zeros((P, 2, P))
    for g in range(2):
        pick[HD1 * g + p % HD1, g, p] = 1.0
    put("kv_pick", pick)
    s, t = p[:, None], p[None, :]
    mask = np.zeros((P, 8, P))
    for n, m in enumerate(LEVELS + (CH,)):
        mask[:, n] = (s // (2 * m) == t // (2 * m)) & (s % (2 * m) < m) & (t % (2 * m) >= m)
    mask[:, 7] = s == t
    freq = np.float32(THETA) ** (-np.arange(0, ROT, 2, dtype=np.float32) / np.float32(ROT))
    col = np.zeros((P, 1), np.float32)
    for head in range(P // HD1):
        for d in range(ROT):
            col[head * HD1 + d, 0] = freq[d % half]
    put("inv_freq", col)
    band = np.full((P, 3, P), NEG)
    band[:, 0][t <= s] = 0.0
    band[:, 1][t > s] = 0.0
    band[:, 2][t <= s] = 0.0
    put("band_mask", band)
    cnt = np.zeros((P, 4, S), np.float32)
    for g, w in enumerate(WINDOWS):
        cnt[:, g] = np.float32(1) / np.minimum(np.arange(S) + 1, w).astype(np.float32)
    scan = np.ones((P, S))
    scan[:, ::CH] = 0.0
    put("chunk_scan", scan)
    dist = np.arange(S)
    exact = BUCKETS // 2
    far = np.maximum(dist, exact).astype(np.float32)
    large = exact + (np.log(far / np.float32(exact)) / np.float32(math.log(MAX_DIST / exact))
                     * np.float32(BUCKETS - exact)).astype(np.int32)
    bucket = np.where(dist < exact, dist, np.minimum(large, BUCKETS - 1))
    hot = np.zeros((BUCKETS, S), np.float32)
    hot[bucket[::-1], np.arange(S)] = 1.0
    return con, hot, mask.reshape(P, -1).astype(np.float32), cnt.reshape(P, -1)


class Job:

    def __init__(self, name, iters, groups, ada=()):
        self.name, self.iters, self.groups, self.ada = name, iters, groups, list(ada)
        self.chunks = [g[2] // KC for g in groups]
        self.offs = [sum(self.chunks[:n]) for n in range(len(groups))]
        self.n = sum(self.chunks)
        self.where = [(g, c) for g in range(len(groups)) for c in range(self.chunks[g])]
        self.ends = {self.offs[g] + self.chunks[g] - 1: g for g in range(len(groups))}
        self.per = self.n + len(self.ada)
        self.at = [p + sum(a < p for a in self.ada) for p in range(self.n)]
        assert iters == 1 or (self.per % RING == 0 and self.n % RING == 0 and len(groups) % 2 == 0)

    def ada_at(self, k):
        p = self.ada[k]
        return self.at[p] + 1 + (k - self.ada.index(p))


def two_block_kernel(nc, xT, params, cons, level_in, count_in, hot_in, rel_bias, pos, w_ada, w_in, w_attn, w_hgrn, w_out,
                     w_ffn_in, w_ffn_out, w_in2, pool_w, w_out2, w_up, w_down, out, stop_after=None):
    ctx = ExitStack()
    with ctx:
        base = (nc.sbuf_base + 31) // 32 * 32
        ctx.enter_context(nc.sbuf_tensor("arena", [P, (nc.sbuf_usable_end - base - 64) // 4], F32))
        limit = nc.sbuf_usable_end
        cursor = [base]

        def place(name, shape, dt=F32, at=None):
            size = int(np.prod(shape[1:])) * (2 if dt == BF16 else 4)
            start = cursor[0] if at is None else at
            if at is None:
                cursor[0] = start + (size + 31) // 32 * 32
            assert start + size <= limit, (name, start + size - limit)
            return nc.alloc_sbuf_tensor_at(name, shape, dt, offset=start)

        par = place("par", [P, NPAR])
        con = place("con", [P, NCON])
        ones = place("ones", [P, P])
        ones_r = place("ones_r", [P, 2], R32)
        ident_bf = place("ident_bf", [P, P], BF16)
        band_bf = place("band_bf", [P, 3 * P], BF16)
        level_mask = place("level_mask", [P, 8 * P])
        inv_count = place("inv_count", [P, 4 * S], at=cursor[0] - 8 * P * 4)
        mod = place("mod", [P, 6 * DT])
        coef = place("coef", [P, 4, DT])
        eps_col = place("eps_col", [P, 2])
        rstd = place("rstd", [P, S])
        lnv = place("lnv", [P, S])
        raw = place("raw", [P, RING, KC, CW])
        w_hi = place("w_hi", [P, RING, KC, CW], R32)
        w_lo = place("w_lo", [P, RING, KC, CW], R32)
        half = place("half", [P, 2, 2, CW])
        X = place("X", [P, DT, 2 * S], R32)
        mx, mx1, negm, den, es = [place(n, [P, 2, 4]) for n in ("mx", "mx1", "negm", "den", "es")]
        lbc = place("lbc", [P, 6, HGH])
        REG = cursor[0]
        KB = 1024

        ada_acc = place("ada_acc", [P, 2, 2, ADA_CB], at=REG)
        ada_hl = place("ada_hl", [P, 2, 2, ADA_CB], R32, at=REG)
        x1 = place("x1", [P, DT, S], at=REG + 56 * KB)
        sq1 = place("sq1", [P, DT, S], at=REG + 72 * KB)
        NP1 = 42
        proj = place("proj", [P, NP1, S], at=REG)
        QA, KA, VA, QH, FH, IH, GH = 0, 8, 9, 10, 18, 26, 34
        T0 = REG + NP1 * KB
        T1 = T0 + 31 * KB
        attn_x = place("attn_x", [P, 8, 2 * S], R32, at=T1)
        hgrn_x = place("hgrn_x", [P, 8, 2 * S], R32, at=T1 + 16 * KB)
        def seq(at, *items):
            outs = []
            for name, shape, dt in items:
                outs.append(place(name, shape, dt, at=at))
                at += (int(np.prod(shape[1:])) * 4 + 31) // 32 * 32
            return outs
        (pos_i, ang, turn_, red, cosk, sink_, cosq, sinq, kr, qr) = seq(
            T0, ("pos_i", [P, S], I32), ("ang", [P, S], F32), ("turn_", [P, S], F32), ("red", [P, S], F32),
            ("cosk", [P, S], F32), ("sink_", [P, S], F32), ("cosq", [P, S], F32), ("sinq", [P, S], F32),
            ("kr", [P, S], F32), ("qr", [P, 2, S], F32))
        (q_cos, q_sin) = seq(T0, ("q_cos", [P, 2, S], F32), ("q_sin", [P, 2, S], F32))
        (probs, probs_t) = seq(T0 + 14 * KB, ("probs", [P, 4, 3 * P], F32), ("probs_t", [P, 4, 3 * P], F32))
        (kd_now, v_now) = seq(T0 + 26 * KB, ("kd_now", [P, S], F32), ("v_now", [P, 2, HD1], F32))
        ada_acc2 = place("ada_acc2", [P, 2, ADA_CB], at=T1 + 16 * KB)
        ada_hl2 = place("ada_hl2", [P, 2, ADA_CB], R32, at=T1 + 16 * KB)
        (kd4, v4) = seq(T1 + 24 * KB, ("kd4", [P, 4, S], F32), ("v4", [P, 4, 2, HD1], F32))
        (decay, Pq, Rk, hg_q, hg_k, hg_v, v_rows, s_ab, s_c, p_c, r_c) = seq(
            T0, ("decay", [P, 8, S], F32), ("Pq", [P, 7, S], F32), ("Rk", [P, 7, S], F32), ("hg_q", [P, S], F32),
            ("hg_k", [P, S], F32), ("hg_v", [P, S], F32), ("v_rows", [P, 2, P], F32), ("s_ab", [P, 2, P], F32),
            ("s_c", [P, P], F32), ("p_c", [P, P], F32), ("r_c", [P, P], F32))
        u_a = place("u_a", [P, 2, CW], at=T0 + 29 * KB)
        hg_l = lnv
        masked = place("masked", [P, 8, P], at=T0)
        hsq = place("hsq", [P, 8, S], at=T0)
        hrs = place("hrs", [P, 8, S], at=T0 + 8 * KB)
        hfull = place("hfull", [P, 8, S], at=T0 + 16 * KB)
        merged = place("merged", [P, DT, 2 * S], R32, at=T0)
        (t_h, u_h, full) = seq(REG + 16 * KB, *[(n, [P, 2, CW], F32) for n in ("t_h", "u_h", "full")])
        ada_acc3 = place("ada_acc3", [P, 2, ADA_CB], at=REG + 24 * KB)
        ada_hl3 = place("ada_hl3", [P, 2, ADA_CB], R32, at=REG + 24 * KB)
        ada_acc4 = place("ada_acc4", [P, 2, ADA_CB], at=REG + 62 * KB)
        ada_hl4 = place("ada_hl4", [P, 2, ADA_CB], R32, at=REG + 62 * KB)
        x_res = place("x_res", [P, DT, S], at=REG + 90 * KB)
        y = place("y", [P, DT, S], at=REG + 74 * KB)
        hid = place("hid", [P, 24, 2 * S], R32, at=REG)
        sq = place("sq", [P, DT, S], at=REG + 48 * KB)
        sq_mix = place("sq_mix", [P, DT, S], at=REG)
        sq_ffn = place("sq_ffn", [P, DT, S], at=REG + 56 * KB)
        (t_g, sg, t_u, fullf) = seq(REG + 48 * KB, *[(n, [P, 2, CW], F32) for n in ("t_g", "sg", "t_u", "fullf")])
        (cu, cacc, csg, cful) = seq(REG + 48 * KB, ("cu", [P, 2, 2, CW + 2], F32), ("cacc", [P, 2, 2, CW], F32),
                                    ("csg", [P, 2, CW], F32), ("cful", [P, 2, CW], F32))
        proj2 = place("proj2", [P, 32, S], at=REG)
        Q2, K2, V2, P2 = 0, 8, 16, 24
        v2_rows = place("v2_rows", [P, 2, 8, P], at=REG + 32 * KB)
        hank = place("hank", [P, 8, S], at=REG + 40 * KB)
        (probs2, probs2_t) = seq(REG + 48 * KB, ("probs2", [P, 4, 3 * P], F32), ("probs2_t", [P, 4, 3 * P], F32))
        sq2 = place("sq2", [P, DT, S], at=REG + 60 * KB)
        (bias_row, hot, relb, mx2, negm2, den2) = seq(REG + 76 * KB, ("bias_row", [P, HANKEL_W], F32), ("hot", [P, S], F32),
                                              ("relb", [P, HEADS2], F32), ("mx2", [P, 2, 4], F32),
                                              ("negm2", [P, 2, 4], F32), ("den2", [P, 2, 4], F32))
        PW = S + 16
        dve_pads = seq(REG + 80 * KB, *[(n, [P, 2, PW], F32) for n in ("pa", "pb_", "pc")])
        pool_pads = seq(REG + 68 * KB, *[(n, [P, 2, PW], F32) for n in ("ga", "gb", "gc")])
        pwt = place("pwt", [P, 4, 2, S], at=REG + 60 * KB)
        pful = place("pful", [P, 8, S], at=REG + 68 * KB)
        hank_dram = nc.dram_tensor("hank_dram", (HEADS2, HANKEL_W), F32, kind="Internal")

        psg = ctx.enter_context(nc.psum_tensor("psg", [P, 4, 512], F32))
        pss = ctx.enter_context(nc.psum_tensor("pss", [P, 4, 512], F32))

        def sem(name):
            return ctx.enter_context(nc.semaphore(name))

        landed = [sem(f"landed{n}") for n in range(RING)]
        raw_used = sem("raw_used")
        hi_ready = sem("hi_ready")
        pe_chunk = sem("pe_chunk")
        half_ready = sem("half_ready")
        ps_free = sem("ps_free")
        par_in, con_in, x_in, misc_in = sem("par_in"), sem("con_in"), sem("x_in"), sem("misc_in")
        ones_set = sem("ones_set")
        x_back = sem("x_back")
        ada_pair, ada_half, ada_split = sem("ada_pair"), sem("ada_half"), sem("ada_split")
        ada_mm, ada_out = sem("ada_mm"), sem("ada_out")
        dve_chain = sem("dve_chain")
        act_chain = sem("act_chain")
        act_parted, sp_parted, pool_parted = sem("act_parted"), sem("sp_parted"), sem("pool_parted")
        gate_ready, full_ready, fhi_ready, opnd_ready = sem("gate_ready"), sem("full_ready"), sem("fhi_ready"), sem("opnd_ready")
        sq_ready, ss_ready, rs_ready, nrm_full, nrm_hi, nrm_out = [sem(n) for n in
            ("sq_ready", "ss_ready", "rs_ready", "nrm_full", "nrm_hi", "nrm_out")]
        y_ready = sem("y_ready")
        out_done = sem("out_done")
        S1 = {n: sem("a1_" + n) for n in ("trig", "tab", "swap", "kr", "dup", "dupo", "vt", "vo", "qswap", "qr",
                                          "s", "mx", "e", "es", "pn", "pt", "pto", "pv", "hi", "lo", "kv_now", "step")}
        SH = {n: sem("hg_" + n) for n in ("act", "prep", "ln", "cp", "d", "exp", "pr", "vt", "vo", "sa", "sb", "ma", "mb",
                                          "sc", "sco", "o", "oo", "sq", "ss", "rs", "full", "hi", "lo", "lbm", "lbe")}
        S2 = {n: sem("a2_" + n) for n in ("sq", "ss", "rs", "qk", "vt", "vo", "row", "rowo", "dr", "hk", "s", "mx", "e",
                                          "pn", "pt", "pto", "pv", "ao", "hi", "lo", "mix", "mixp", "step", "pw", "pwm", "pfu", "phi", "plo")}
        gate_half, level_ld = sem("gate_half"), sem("level_ld")
        local, hl, mul_done, add_done, cmid = [sem(n) for n in ("dve_local", "hg_local", "mul_done", "add_done", "cmid")]
        SC = {n: sem("cv_" + n) for n in ("zero", "aff", "acc")}

        def col(i, c0, step):
            return c0 + i * step

        def wide(W, k0, kt, c0, step=0):
            return (W.rearrange("(k p) n -> p k n", p=P), k0, kt, c0, step)

        GATE_A, GATE_H = NP1 * P, NP1 * P + D

        def spread(n):
            return [3 + k * (n - 3) // DT for k in range(DT)]
        jobs = [
            Job("kv", 1, [wide(w_in, 0, DT, KA * P)]),
            Job("qa", 2, [wide(w_in, 0, DT, 0, 2 * CW), wide(w_in, 0, DT, CW, 2 * CW)]),
            Job("hg", 4, [wide(w_in, 0, DT, t * P, CW) for t in (QH, FH, IH, GH)], spread(16)),
            Job("m1", 4, [wide(w_in, 0, DT, GATE_A, 2 * CW), wide(w_attn, 0, 8, 0, 2 * CW),
                          wide(w_in, 0, DT, GATE_A + CW, 2 * CW), wide(w_attn, 0, 8, CW, 2 * CW)]),
            Job("m2", 4, [wide(w_in, 0, DT, GATE_H, 2 * CW), wide(w_hgrn, 0, 8, 0, 2 * CW),
                          wide(w_in, 0, DT, GATE_H + CW, 2 * CW), wide(w_hgrn, 0, 8, CW, 2 * CW)]),
            Job("out", 2, [wide(w_out, 0, DT, n * CW, 4 * CW) for n in range(4)], spread(16)),
            Job("up1a", 12, [wide(w_ffn_in, 0, DT, 0, CW), wide(w_ffn_in, 0, DT, HID, CW)]),
            Job("dn1a", 2, [wide(w_ffn_out, 0, 24, n * CW, 4 * CW) for n in range(4)], spread(24)),
            Job("up1b", 10, [wide(w_ffn_in, 0, DT, 12 * CW, CW), wide(w_ffn_in, 0, DT, HID + 12 * CW, CW)]),
            Job("dn1b", 2, [wide(w_ffn_out, 24, 20, n * CW, 4 * CW) for n in range(4)]),
            Job("in2", 4, [wide(w_in2, 0, DT, 0, 2 * CW), wide(w_in2, 0, DT, CW, 2 * CW)]),
            Job("in2v", 2, [wide(w_in2, 0, DT, 8 * CW, 2 * CW), wide(w_in2, 0, DT, 9 * CW, 2 * CW)]),
            Job("in2p", 2, [wide(w_in2, 0, DT, 12 * CW, 2 * CW), wide(w_in2, 0, DT, 13 * CW, 2 * CW)]),
            Job("out2", 4, [wide(w_out2, 0, DT, 0, 2 * CW), wide(w_out2, 0, DT, CW, 2 * CW)]),
            Job("up2a", 12, [wide(w_up, 0, DT, 0, CW), wide(w_up, 0, DT, HID, CW)]),
            Job("dn2a", 4, [wide(w_down, 0, 24, 0, 2 * CW), wide(w_down, 0, 24, CW, 2 * CW)]),
            Job("up2b", 10, [wide(w_up, 0, DT, 12 * CW, CW), wide(w_up, 0, DT, HID + 12 * CW, CW)]),
            Job("dn2b", 2, [wide(w_down, 24, 20, n * CW, 4 * CW) for n in range(4)]),
        ]
        ADA_FIRST = 4
        ADA_CHUNKS = ADA_FIRST * DT
        r, h, G, m = ADA_CHUNKS + RING, 0, 0, ADA_FIRST
        for n, j in enumerate(jobs):
            j.r0, j.h0, j.G0, j.m0 = r, h, G, m
            j.next = jobs[n + 1] if n + 1 < len(jobs) else None
            j.prev = jobs[n - 1] if n else None
            r += j.iters * j.per
            h += j.iters * j.n
            G += j.iters * len(j.groups)
            m += j.iters if j.ada else 0
        J = {j.name: j for j in jobs}

        def landing(j, i, k):
            return j.r0 + i * j.per + k

        def slot_of(j, k):
            return (j.r0 + k) % RING

        def landed_at(j, i, k):
            return 16 * ((j.r0 + k) // RING + 1) + i * (16 * j.per // RING)

        def ahead(j, i, p, final):
            q = p + RING
            if q < j.n:
                return j, i, q
            if not final:
                return j, i + 1, q - j.n
            return (j.next, 0, q - j.n) if j.next is not None else None

        def half_slot(j, q):
            return (j.h0 + q) % RING

        def landing_of(j, i, q):
            if q >= RING:
                return landing(j, i, j.at[q - RING])
            if not is_first(i):
                return landing(j, i - 1, j.at[j.n - RING + q])
            if j.prev is None:
                return ADA_CHUNKS + q
            return landing(j.prev, j.prev.iters - 1, j.prev.at[j.prev.n - RING + q])

        def group_no(j, i, g):
            return j.G0 + i * len(j.groups) + g

        def bank_of(j, g):
            return 2 * ((j.G0 + g) % 2)

        def chunks_done(j, i, g):
            return j.h0 + i * j.n + j.offs[g] + j.chunks[g]

        def sums_done(j, i, g):
            return group_no(j, i, g) + 2

        def all_sums(j):
            return sums_done(j, j.iters - 1, len(j.groups) - 1)

        def w_src(j, i, q):
            g, c = j.where[q]
            W, k0, kt, c0, step = j.groups[g]
            return W[:, k0 + c * KC:k0 + (c + 1) * KC, ds(c0 + i * step, CW)]

        def is_static(v):
            return isinstance(v, int)

        def is_first(v):
            return is_static(v) and v == 0

        def turns(eng, n, body):
            body(0)
            if n == 2:
                body(1)
            elif n > 2:
                with eng.Fori(1, n) as i:
                    body(i)

        def all_turns(eng, j, body, peel=False):
            if peel and j.iters > 2:
                body(j, 0, False)
                with eng.Fori(1, j.iters - 1) as i:
                    body(j, i, False)
            elif j.iters == 2:
                body(j, 0, False)
            elif j.iters > 2:
                with eng.Fori(0, j.iters - 1) as i:
                    body(j, i, False)
            body(j, j.iters - 1, True)

        RUN = [j.name for j in jobs]
        if stop_after is not None:
            RUN = RUN[:RUN.index(stop_after) + 1] if stop_after in RUN else []
        live = [J[n] for n in RUN]
        for j in live:
            if j.next is not None and j.next.name not in RUN:
                j.next = None

        def runs(name):
            return name in RUN

        def flat3(a):
            return a.rearrange("p t s -> p (t s)")

        def flat(a):
            return flat3(a[:, :, :])

        def pooled(eng, step, g, pads):
            p2 = proj2[:, P2 + 2 * g:P2 + 2 * g + 2, :]
            a, b, c = pads
            for z in pads:
                eng.memset(z[:, :, 0:16], 0.0)
            step(eng.tensor_copy(a[:, :, 16:], p2))
            src, dst, width = a, b, 1
            for _ in range(g + 1):
                step(eng.tensor_tensor(dst[:, :, 2 * width - 1:], src[:, :, 2 * width - 1:],
                                       src[:, :, width - 1:PW - width], ALU.add))
                src, dst, width = dst, (c if dst is b else b), 2 * width
            cnt = inv_count[:, g * S:(g + 1) * S][:, None, :].broadcast_to((P, 2, S))
            step(eng.tensor_tensor(a[:, :, 16:], src[:, :, 16:], cnt, ALU.mult))
            return eng.tensor_tensor(p2, a[:, :, 16:], p2, ALU.subtract)

        block = ctx.enter_context(nc.Block())

        def P_(name, a=0, b=None):
            lo, hi = PAR[name]
            return par[:, lo + a:(hi if b is None else lo + b)]

        def C_(name, a=0, b=None):
            lo, hi = CON[name]
            return con[:, lo + a:(hi if b is None else lo + b)]

        @block.sync
        def _(sp):
            sp.dma_start(par[:, :], params).then_inc(par_in, 16)
            sp.dma_start(x1[:, :, :], xT.rearrange("(t p) s -> p t s", p=P)).then_inc(x_in, 16)
            sp.dma_start(con[:, :], cons).then_inc(con_in, 16)
            ada_v = w_ada.rearrange("(k p) n -> p k n", p=P)

            def ada_turn(i):
                for cb in range(2):
                    for k in range(DT):
                        n = cb * DT + k
                        if not (is_first(i) and n < RING):
                            sp.wait_ge(raw_used, i * 2 * DT + n - RING + 1)
                        sp.dma_start(raw[:, n % RING, :, :].rearrange("p k n -> p (k n)"),
                                     ada_v[:, k, ds(i * 2 * ADA_CB + cb * ADA_CB, ADA_CB)]
                                     ).then_inc(landed[n % RING], 16)
            turns(sp, ADA_FIRST // 2, ada_turn)
            for q in range(RING if live else 0):
                sp.wait_ge(raw_used, ADA_CHUNKS + q - RING + 1)
                sp.dma_start(raw[:, q, :, :], w_src(jobs[0], 0, q)).then_inc(landed[q], 16)

            def load(j, i, k, src, flat_=False):
                s = slot_of(j, k)
                sp.wait_ge(raw_used, landing(j, i, k) - RING + 1)
                if not is_static(i):
                    sp.sem_inc(sp_parted, 1)
                dst = raw[:, s, :, :].rearrange("p k n -> p (k n)") if flat_ else raw[:, s, :, :]
                sp.dma_start(dst, src).then_inc(landed[s], 16)

            def job_turn(j, i, final):
                for p in range(j.n):
                    nxt = ahead(j, i, p, final)
                    if nxt:
                        load(j, i, j.at[p], w_src(*nxt))
                    for k, a in enumerate(j.ada):
                        if a == p:
                            load(j, i, j.ada_at(k), ada_v[:, k, ds((j.m0 + i) * ADA_CB, ADA_CB)], True)
            for j in live:
                all_turns(sp, j, job_turn)
        def bcast_rows(a):
            return bass.AP(tensor=a.tensor, offset=a.offset, ap=[[0, P], [1, S]])

        def shifted_rows(h):
            return bass.AP(tensor=h, offset=0, ap=[[1, P], [HANKEL_W, HEADS2], [1, S]])


        @block.gpsimd
        def _(pool):
            pool.dma_start(pos_i[:, :], bcast_rows(pos)).then_inc(misc_in, 16)
            pool.dma_start(level_mask[:, :], level_in).then_inc(level_ld, 16)

            def ada_pairs(acc, hl_, m, used):
                pool.wait_ge(raw_used, used)
                nc.gpsimd.tensor_tensor(acc[:, 0, :], acc[:, 0, :], acc[:, 1, :], ALU.add).then_inc(ada_pair, 1)
                pool.wait_ge(ada_pair, m + 1)
                pool.sem_inc(pool_parted, 1)
                nc.gpsimd.tensor_copy(hl_[:, 1, :], acc[:, 0, :]).then_inc(ada_half, 1)
                pool.wait_ge(ada_half, m + 1)
                nc.gpsimd.tensor_tensor(hl_[:, 0, :], acc[:, 0, :], hl_[:, 1, :].bitcast(F32), ALU.subtract
                                        ).then_inc(ada_split, 1)

            def ada_job(j, acc, hl_):
                def turn(i):
                    ada_pairs(acc, hl_, j.m0 + i, landing(j, i, j.ada_at(15)) + 1)
                turns(pool, j.iters, turn)

            def ada_turn(i):
                for cb in range(2):
                    ada_pairs(ada_acc[:, cb, :, :], ada_hl[:, cb, :, :], i * 2 + cb, (i * 2 + cb + 1) * DT)
            turns(pool, ADA_FIRST // 2, ada_turn)
            if runs("hg"):
                ada_job(J["hg"], ada_acc2, ada_hl2)
            if runs("out"):
                pool.wait_ge(pe_chunk, chunks_done(J["m2"], J["m2"].iters - 1, 3))
                pool.dma_start(x_res[:, :, :], xT.rearrange("(t p) s -> p t s", p=P)).then_inc(x_back, 16)
                pool.wait_ge(SH["mb"], HGH + 1)
                pool.dma_start(inv_count[:, :], count_in).then_inc(level_ld, 16)
                ada_job(J["out"], ada_acc3, ada_hl3)
            if runs("dn1a"):
                ada_job(J["dn1a"], ada_acc4, ada_hl4)
            if runs("in2"):
                pool.wait_ge(pe_chunk, chunks_done(J["dn1b"], 1, 3))
                pool.wait_ge(nrm_out, 12)
                pool.dma_start(hot[0:BUCKETS, :], hot_in).then_inc(misc_in, 16)
                pool.dma_start(relb[0:BUCKETS, :], rel_bias).then_inc(misc_in, 16)
                pool.wait_ge(S2["rowo"], 2)
                pool.dma_start(hank_dram.ap(), bias_row[0:HEADS2, :]).then_inc(S2["dr"], 16)
                pool.wait_ge(S2["dr"], 16)
                pool.dma_start(hank[:, :, :], shifted_rows(hank_dram)).then_inc(S2["hk"], 16)
                pool.wait_ge(S2["qk"], 2)
                pool.dma_start(pwt[:, :, :, :], pool_w.rearrange("g (k p) n -> p g k n", p=P)).then_inc(S2["pw"], 16)
                pool.wait_ge(level_ld, 32)
                pool.wait_ge(ps_free, sums_done(J["in2p"], 0, 1))
                steps = [0]

                def step(ins):
                    ins.then_inc(S2["step"], 1)
                    steps[0] += 1
                    pool.wait_ge(S2["step"], steps[0])
                for g in range(2):
                    pooled(nc.gpsimd, step, g, pool_pads).then_inc(S2["mixp"], 1)
                    pool.wait_ge(S2["mixp"], g + 1)
            if runs("dn2b"):
                for q in range(4):
                    pool.wait_ge(y_ready, 9 + q)
                    pool.dma_start(out.rearrange("(t p) s -> p t s", p=P)[:, 4 * q:4 * q + 4, :],
                                   x_res[:, 4 * q:4 * q + 4, :]).then_inc(out_done, 16)
                pool.wait_ge(out_done, 64)

        @block.scalar
        def _(act):
            chain = [0]

            def link(ins):
                ins.then_inc(act_chain, 1)
                chain[0] += 1
                act.wait_ge(act_chain, chain[0])

            def apart():
                act.sem_inc(act_parted, 1)

            def split_first():
                for q in range(RING):
                    act.wait_ge(landed[q], 16 * (ADA_CHUNKS // RING + 1))
                    nc.scalar.activation(w_hi[:, q, :, :], raw[:, q, :, :], ACT.Copy).then_inc(hi_ready, 1)

            def take_half(j, i, g):
                b = bank_of(j, g)
                act.wait_ge(pe_chunk, chunks_done(j, i, g))
                if group_no(j, 0, g) > 0:
                    act.wait_ge(ps_free, sums_done(j, i, g) - 2)
                nc.scalar.activation(half[:, b // 2, :, :], psg[:, b:b + 2, CW:2 * CW], ACT.Copy).then_inc(half_ready, 1)

            def job(j, after=None, side=None, funcs=None):
                if funcs:
                    act.preload_act_table(funcs)

                def turn(j, i, final):
                    for p in range(j.n):
                        nxt = ahead(j, i, p, final)
                        if nxt:
                            k = j.at[p]
                            act.wait_ge(landed[slot_of(j, k)], landed_at(j, i, k))
                            act.wait_ge(pe_chunk, j.h0 + i * j.n + p + 1)
                            nc.scalar.activation(w_hi[:, half_slot(j, p), :, :], raw[:, slot_of(j, k), :, :], ACT.Copy
                                                 ).then_inc(hi_ready, 1)
                        if side:
                            side(i, p, final)
                        if p in j.ends:
                            g = j.ends[p]
                            take_half(j, i, g)
                            if after:
                                after(i, g)
                all_turns(act, j, turn)

            nrm = [0]

            def norm_stats(src, sqb, extra=None, qs=range(4)):
                k = nrm[0]
                for q in qs:
                    if extra:
                        extra(q)
                    nc.scalar.activation(sqb[:, 4 * q:4 * q + 4, :], src[:, 4 * q:4 * q + 4, :], ACT.Square
                                         ).then_inc(sq_ready, 1)
                act.wait_ge(ss_ready, k + 1)
                link(nc.scalar.activation(lnv[:, :], pss[:, 0, 0:S], ACT.Ln, scale=1.0 / D, bias=eps_col[:, 0:1]))
                nc.scalar.activation(rstd[:, :], lnv[:, :], ACT.Exp, scale=-0.5).then_inc(rs_ready, 1)
                nrm[0] += 1

            def early_squares(sqb, stored):
                def after(i, g):
                    if i == 1 and g in (0, 2):
                        stored(i, g)
                        for q in ((0, 1) if g == 0 else (2,)):
                            nc.scalar.activation(sqb[:, 4 * q:4 * q + 4, :], y[:, 4 * q:4 * q + 4, :], ACT.Square
                                                 ).then_inc(sq_ready, 1)
                return after

            opn = [0]

            def norm_operand(fullb):
                for q in range(4):
                    act.wait_ge(nrm_full, 4 * opn[0] + q + 1)
                    nc.scalar.activation(X[:, 4 * q:4 * q + 4, 0:S], fullb[:, 4 * q:4 * q + 4, :], ACT.Copy
                                         ).then_inc(nrm_hi, 1)
                opn[0] += 1

            act.wait_ge(ones_set, 1)
            act.wait_ge(x_in, 16)
            norm_stats(x1, sq1)
            act.wait_ge(SH["lbm"], 1)
            nc.scalar.activation(lbc[:, 1:3, :], lbc[:, 1:3, :], ACT.Exp).then_inc(SH["lbe"], 1)
            act.wait_ge(S1["trig"], 2)
            nc.scalar.activation(sink_[:, :], red[:, :], ACT.Sin).then_inc(S1["tab"], 1)
            nc.scalar.activation(cosk[:, :], turn_[:, :], ACT.Sin).then_inc(S1["tab"], 1)
            if live:
                split_first()
            norm_operand(sq1)

            if runs("kv"):
                job(J["kv"])

                def side(i, p, final):
                    if not final:
                        return
                    if p == 1:
                        act.wait_ge(S1["vt"], 1)
                        for b in range(4):
                            g = pss[:, 2, 0:S].rearrange("p (a g d) -> p g a d", a=2, g=2)[:, b // 2]
                            ins = nc.scalar.activation(v4[:, b, :, :], g, ACT.Copy)
                        ins.then_inc(S1["vo"], 1)
                    if p == 3:
                        act.wait_ge(S1["dup"], 2)
                        for b in range(4):
                            g = b // 2
                            ins = nc.scalar.activation(kd4[:, b, :], pss[:, 1, g * S:(g + 1) * S], ACT.Copy)
                        ins.then_inc(S1["dupo"], 1)
                job(J["qa"], side=side)

            if runs("hg"):
                act.wait_ge(S1["dupo"], 1)
                act.wait_ge(S1["vo"], 1)

                def side(b, p, final):
                    if p == 1:
                        act.wait_ge(S1["pv"], b + 1)
                        apart()
                        nc.scalar.activation(kd_now[:, :], kd4[:, ds(b, 1), :].rearrange("p a s -> p (a s)"), ACT.Copy)
                        nc.scalar.activation(v_now[:, :, :].rearrange("p a d -> p (a d)"),
                                             v4[:, ds(b, 1), :, :].rearrange("p b a d -> p (b a d)"), ACT.Copy
                                             ).then_inc(S1["kv_now"], 1)
                    if p in (6, 7):
                        if p == 6:
                            act.wait_ge(S1["mx"], b + 1)
                        for hh in ((0, 1) if p == 6 else (2, 3)):
                            nc.scalar.activation(probs[:, hh, 0:P], pss[:, hh, 0:P], ACT.Exp, bias=negm[:, 0, hh:hh + 1],
                                                 accum_out=den[:, 0, hh:hh + 1])
                            nc.scalar.activation(probs[:, hh, P:3 * P], pss[:, hh, P:3 * P], ACT.Exp,
                                                 bias=negm[:, 1, hh:hh + 1], accum_out=den[:, 1, hh:hh + 1]
                                                 ).then_inc(S1["e"], 1)
                        if p == 7:
                            nc.scalar.activation(es[:, :, :], es[:, :, :], ACT.Exp).then_inc(S1["es"], 1)
                    if p == 12:
                        act.wait_ge(S1["pt"], b + 1)
                        nc.scalar.activation(probs_t[:, :, :], pss[:, :, 0:3 * P], ACT.Copy).then_inc(S1["pto"], 1)
                    if p == 14:
                        act.wait_ge(S1["pv"], b + 2)
                        apart()
                        nc.scalar.activation(attn_x[:, ds(2 * b, 2), 0:S], pss[:, 0, :].rearrange("p (a s) -> p a s", a=2),
                                             ACT.Copy).then_inc(S1["hi"], 1)

                def after(i, g):
                    if g == 2:
                        return
                    act.wait_ge(ps_free, sums_done(J["hg"], i, g))
                    apart()
                    t = proj[:, ds((QH, FH, IH, GH)[g] + 2 * i, 2), :]
                    nc.scalar.activation(t, t, ACT.Silu if g == 0 else ACT.Sigmoid).then_inc(SH["act"], 1)
                job(J["hg"], after, side)

            if runs("m1"):
                act.preload_act_table_set("natural_log_exp_and_others")
                act.wait_ge(S1["lo"], 5)
                act.sem_inc(SH["oo"], 1)
                act.wait_ge(SH["prep"], 4)

                def side(i, p, final):
                    h, q = 2 * i + p // 6, p % 6
                    if q == 0:
                        act.wait_ge(SH["sb"], h + 1)
                        act.wait_ge(SH["mb"], h + 1)
                        apart()
                        nc.scalar.activation(hg_l[:, :], proj[:, ds(FH + h, 1), :].rearrange("p a s -> p (a s)"), ACT.Ln,
                                             bias=eps_col[:, 1:2]).then_inc(SH["ln"], 1)
                        nc.scalar.activation(hg_q[:, :], proj[:, ds(QH + h, 1), :].rearrange("p a s -> p (a s)"), ACT.Copy
                                             ).then_inc(SH["cp"], 1)
                        nc.scalar.activation(hg_v[:, :], proj[:, ds(IH + h, 1), :].rearrange("p a s -> p (a s)"), ACT.Copy
                                             ).then_inc(SH["cp"], 1)
                    if q == 1:
                        act.wait_ge(SH["d"], h + 1)
                        nc.scalar.activation(decay[:, :, :], decay[:, :, :], ACT.Exp).then_inc(SH["exp"], 1)
                        act.wait_ge(SH["vt"], h + 1)
                        nc.scalar.activation(v_rows[:, :, :].rearrange("p a s -> p (a s)"), pss[:, 0, 0:S], ACT.Copy
                                             ).then_inc(SH["vo"], 1)
                    if q == 5:
                        act.wait_ge(SH["sc"], h + 1)
                        nc.scalar.activation(s_c[:, :], pss[:, 0, 0:P], ACT.Copy).then_inc(SH["sco"], 1)
                        act.wait_ge(SH["o"], h + 2)
                        apart()
                        nc.scalar.activation(proj[:, ds(IH + h, 1), :].rearrange("p a s -> p (a s)"), pss[:, 2, 0:S], ACT.Copy
                                             ).then_inc(SH["oo"], 1)

                def after(i, g):
                    if g % 2 == 0:
                        act.wait_ge(ps_free, sums_done(J["m1"], i, g))
                        apart()
                        t = proj[:, ds(4 * i + g, 2), :]
                        nc.scalar.activation(t, t, ACT.Tanh, scale=0.5).then_inc(gate_ready, 1)
                job(J["m1"], after, side)
                act.wait_ge(SH["oo"], HGH + 1)
                nc.scalar.activation(hsq[:, :, :], proj[:, IH:IH + 8, :], ACT.Square).then_inc(SH["sq"], 1)
                act.wait_ge(SH["ss"], 1)
                link(nc.scalar.activation(hrs[:, :, :].rearrange("p t s -> p (t s)"), pss[:, :, :].rearrange("p t s -> p (t s)"),
                                          ACT.Ln, scale=1.0 / P, bias=eps_col[:, 0:1]))
                nc.scalar.activation(hrs[:, :, :], hrs[:, :, :], ACT.Exp, scale=-0.5).then_inc(SH["rs"], 1)
                act.wait_ge(SH["full"], 1)
                nc.scalar.activation(hgrn_x[:, :, 0:S], hfull[:, :, :], ACT.Copy).then_inc(SH["hi"], 1)

            if runs("m2"):
                def after(i, g):
                    n = 2 * i + g // 2
                    if g % 2 == 0:
                        act.wait_ge(ps_free, sums_done(J["m2"], i, g))
                        nc.scalar.activation(t_h[:, :, :], t_h[:, :, :], ACT.Sigmoid).then_inc(gate_ready, 1)
                    else:
                        act.wait_ge(full_ready, n + 1)
                        apart()
                        nc.scalar.activation(merged[:, ds(2 * n, 2), 0:S], full[:, :, :], ACT.Copy).then_inc(fhi_ready, 1)
                job(J["m2"], after, None, ACT.Sigmoid)

            def swiglu_after(j, tb, sb, fb, k0):
                def after(i, g):
                    if g == 0:
                        act.wait_ge(ps_free, sums_done(j, i, g))
                        nc.scalar.activation(sb[:, :, :], tb[:, :, :], ACT.Silu).then_inc(gate_ready, 1)
                    else:
                        act.wait_ge(full_ready, k0 + i + 1)
                        apart()
                        nc.scalar.activation(hid[:, ds(2 * i, 2), 0:S], fb[:, :, :], ACT.Copy).then_inc(fhi_ready, 1)
                return after

            def conv_after(j, k0):
                def after(i, g):
                    act.wait_ge(ps_free, sums_done(j, i, g))
                    apart()
                    t0 = (24 if j.name == "up2b" else 0) + (HIDT if g else 0)
                    for a in range(2):
                        o = PAR["conv_w_2"][0] + 2 * 2 * HIDT + t0 + a
                        ob = PAR["conv_b_2"][0] + t0 + a
                        nc.scalar.activation(cacc[:, g, a, :], cu[:, g, a, 2:], ACT.Identity,
                                             scale=par[:, ds(2 * i + o, 1)], bias=par[:, ds(2 * i + ob, 1)]
                                             ).then_inc(SC["aff"], 1)
                    if g == 0:
                        act.wait_ge(SC["acc"], 2 * (k0 + i) + 1)
                        nc.scalar.activation(csg[:, :, :], cacc[:, 0, :, :], ACT.Silu).then_inc(gate_ready, 1)
                    else:
                        act.wait_ge(full_ready, 30 + k0 + i + 1)
                        apart()
                        nc.scalar.activation(hid[:, ds(2 * i, 2), 0:S], cful[:, :, :], ACT.Copy).then_inc(fhi_ready, 1)
                return after

            if runs("out"):
                job(J["out"], early_squares(sq_mix, lambda i, g: act.wait_ge(ps_free, sums_done(J["out"], i, g))))
                act.wait_ge(ps_free, all_sums(J["out"]))
                norm_stats(y, sq_mix, None, (3,))
                norm_stats(x_res, sq, lambda q: act.wait_ge(y_ready, q + 1))
                norm_operand(sq)
            if runs("up1a"):
                job(J["up1a"], swiglu_after(J["up1a"], t_g, sg, fullf, 8), None, ACT.Silu)
                job(J["dn1a"])
                job(J["up1b"], swiglu_after(J["up1b"], t_g, sg, fullf, 20), None, ACT.Silu)
                job(J["dn1b"], early_squares(sq_ffn, lambda i, g: act.wait_ge(add_done, 4 * i + g + 1)))
                act.wait_ge(add_done, 8)
                norm_stats(y, sq_ffn, None, (3,))
                norm_stats(x_res, sq, lambda q: act.wait_ge(y_ready, 4 + q + 1))
                norm_operand(sq)

            if runs("in2"):
                job(J["in2"])

                def side(i, p, final):
                    if p == 0:
                        act.wait_ge(ps_free, all_sums(J["in2"]))
                        nc.scalar.activation(sq2[:, 8 * i:8 * i + 8, :], proj2[:, 8 * i:8 * i + 8, :], ACT.Square
                                             ).then_inc(S2["sq"], 1)
                    if p == 3:
                        act.wait_ge(S2["ss"], i + 1)
                        link(nc.scalar.activation(flat3(sq2[:, 8 * i:8 * i + 8, :]), flat3(pss[:, :, :]), ACT.Ln,
                                                  scale=1.0 / P, bias=eps_col[:, 0:1]))
                        nc.scalar.activation(sq2[:, 8 * i:8 * i + 8, :], sq2[:, 8 * i:8 * i + 8, :], ACT.Exp, scale=-0.5
                                             ).then_inc(S2["rs"], 1)
                job(J["in2v"], None, side)

                def heads_out(b):
                    act.wait_ge(S2["pv"], b + 1)
                    nc.scalar.activation(proj2[:, V2 + 4 * b:V2 + 4 * b + 4, :],
                                         pss[:, 0:2, :].rearrange("p t (a s) -> p (t a) s", a=2), ACT.Copy).then_inc(S2["ao"], 1)

                def side(b, p, final):
                    if p == 1 and b == 0:
                        act.wait_ge(S2["vt"], 1)
                        nc.scalar.activation(v2_rows[:, :, :, :].rearrange("p a h d -> p (a h d)"), flat3(pss[:, :, :]), ACT.Copy
                                             ).then_inc(S2["vo"], 1)
                    if p == 1 and b == 1:
                        heads_out(0)
                    if p == 4:
                        act.wait_ge(S2["mx"], b + 1)
                        for hh in range(4):
                            nc.scalar.activation(probs2[:, hh, 0:P], pss[:, hh, 0:P], ACT.Exp, bias=negm2[:, 0, hh:hh + 1],
                                                 accum_out=den2[:, 0, hh:hh + 1])
                            nc.scalar.activation(probs2[:, hh, P:3 * P], pss[:, hh, P:3 * P], ACT.Exp,
                                                 bias=negm2[:, 1, hh:hh + 1], accum_out=den2[:, 1, hh:hh + 1]
                                                 ).then_inc(S2["e"], 1)
                    if p == 7:
                        act.wait_ge(S2["pt"], b + 1)
                        nc.scalar.activation(probs2_t[:, :, :], pss[:, :, 0:3 * P], ACT.Copy).then_inc(S2["pto"], 1)
                job(J["in2p"], None, side)
                heads_out(1)
                act.wait_ge(S2["ao"], 2)
                act.wait_ge(pe_chunk, J["in2p"].h0 + 2 * J["in2p"].n)
                nc.scalar.activation(X[:, 0:8, 0:S], proj2[:, V2:V2 + 8, :], ACT.Copy).then_inc(S2["hi"], 1)
                act.wait_ge(S2["pwm"], 1)
                for t in range(8):
                    ins = nc.scalar.activation(pful[:, t, :], pss[:, t // 2, (t % 2) * S:(t % 2 + 1) * S], ACT.Copy,
                                               scale=P_("pool_scale_2", t, t + 1))
                ins.then_inc(S2["pfu"], 1)
                act.wait_ge(S2["pfu"], 1)
                nc.scalar.activation(X[:, 8:16, 0:S], pful[:, :, :], ACT.Copy).then_inc(S2["phi"], 1)
            if runs("out2"):
                job(J["out2"])
                act.wait_ge(add_done, 16)
                norm_stats(x_res, sq)
                norm_operand(sq)
            if runs("up2a"):
                job(J["up2a"], conv_after(J["up2a"], 0), None, ACT.Silu)
                job(J["dn2a"])
                job(J["up2b"], conv_after(J["up2b"], 12), None, ACT.Silu)
                job(J["dn2b"])

        @block.vector
        def _(dve):
            chain = [0]

            def link(ins):
                ins.then_inc(dve_chain, 1)
                chain[0] += 1
                dve.wait_ge(dve_chain, chain[0])

            ln = [0]

            def here(ins):
                ins.then_inc(local, 1)
                ln[0] += 1
                dve.wait_ge(local, ln[0])

            def split_first():
                for q in range(RING):
                    dve.wait_ge(hi_ready, q + 1)
                    nc.vector.tensor_tensor(w_lo[:, q, :, :], raw[:, q, :, :], w_hi[:, q, :, :].bitcast(F32),
                                            ALU.subtract).then_inc(raw_used, 1)

            def take_sum(j, i, g, dst):
                b = bank_of(j, g)
                dve.wait_ge(half_ready, group_no(j, i, g) + 1)
                nc.vector.tensor_tensor(dst, psg[:, b:b + 2, 0:CW], half[:, b // 2, :, :], ALU.add).then_inc(ps_free, 1)

            def ada_step(acc, s, landed_n, used_n, k):
                w = raw[:, s, :, :].rearrange("p k n -> p (k n)")
                ck = P_("c", k, k + 1)
                if k >= 2:
                    dve.wait_ge(raw_used, used_n)
                dve.wait_ge(landed[s], landed_n)
                if k < 2:
                    nc.vector.tensor_scalar(acc[:, k % 2, :], w, ck, None, ALU.mult).then_inc(raw_used, 1)
                else:
                    nc.vector.scalar_tensor_tensor(acc[:, k % 2, :], w, ck, acc[:, k % 2, :], ALU.mult, ALU.add
                                                   ).then_inc(raw_used, 1)

            def ada_result(m):
                dve.wait_ge(ada_mm, m + 1)
                nc.vector.tensor_tensor(mod[:, ds(m * 8, 8)], pss[:, 3, 496:512:2],
                                        par[:, ds(m * 8 + PAR["b_ada"][0], 8)], ALU.add).then_inc(ada_out, 1)

            def job(j, dest, after=None, side=None, acc=None):
                def turn(j, i, final):
                    for p in range(j.n):
                        nxt = ahead(j, i, p, final)
                        if nxt:
                            dve.wait_ge(hi_ready, j.h0 + i * j.n + p + RING + 1)
                            hs = half_slot(j, p)
                            nc.vector.tensor_tensor(w_lo[:, hs, :, :], raw[:, slot_of(j, j.at[p]), :, :],
                                                    w_hi[:, hs, :, :].bitcast(F32), ALU.subtract).then_inc(raw_used, 1)
                        if j.ada and p == 3 and not is_first(i):
                            ada_result(j.m0 + i - 1)
                        for k, a in enumerate(j.ada):
                            if a == p:
                                n = j.ada_at(k)
                                if k == 0:
                                    dve.wait_ge(ada_mm, j.m0 + i)
                                back = landing(j, i, j.ada_at(k - 2)) + 1 if k >= 2 else None
                                ada_step(acc, slot_of(j, n), landed_at(j, i, n), back, k)
                        if side:
                            side(i, p, final)
                        if p in j.ends:
                            g = j.ends[p]
                            take_sum(j, i, g, dest(i, g))
                            if after:
                                after(i, g)
                all_turns(dve, j, turn, bool(j.ada))
                if j.ada:
                    ada_result(j.m0 + j.iters - 1)

            def bc(ap, shape):
                return ap.broadcast_to(shape)

            nrm = [0]

            def norm_operand(src, fullb, A, B):
                k = nrm[0]
                dve.wait_ge(rs_ready, rsn[0])
                for q in range(4):
                    t = slice(4 * q, 4 * q + 4)
                    here(nc.vector.tensor_tensor(fullb[:, t, :], src[:, t, :], mid(rstd[:, :], 4), ALU.mult))
                    for a in range(4):
                        n = 4 * q + a
                        ins = nc.vector.tensor_scalar(fullb[:, n, :], fullb[:, n, :], A[:, n:n + 1],
                                                      B[:, n:n + 1] if B is not None else None,
                                                      ALU.mult, ALU.add if B is not None else ALU.bypass)
                    ins.then_inc(nrm_full, 1)
                    dve.wait_ge(nrm_hi, 4 * k + q + 1)
                    nc.vector.tensor_tensor(X[:, t, S:2 * S], fullb[:, t, :], X[:, t, 0:S].bitcast(F32), ALU.subtract
                                            ).then_inc(nrm_out, 1)
                nrm[0] += 1

            rsn = [0]

            def mid(ap, n):
                return ap[:, None, :].broadcast_to((P, n, ap.shape[-1]))

            def last(ap, n):
                return ap[..., None].broadcast_to(tuple(ap.shape) + (n,))

            nc.vector.memset(eps_col[:, 0:1], EPS).then_inc(ps_free, 1)
            nc.vector.memset(eps_col[:, 1:2], TINY).then_inc(SH["mb"], 1)
            nc.vector.memset(ones[:, :], 1.0).then_inc(ones_set, 1)
            dve.wait_ge(ones_set, 1)
            nc.vector.tensor_copy(ones_r[:, :], ones[:, 0:2]).then_inc(ones_set, 1)
            dve.wait_ge(con_in, 16)
            nc.vector.tensor_copy(ident_bf[:, :], C_("ident")).then_inc(S1["lo"], 1)
            nc.vector.tensor_copy(band_bf[:, :], C_("band_mask")).then_inc(ones_set, 1)
            dve.wait_ge(par_in, 16)
            here(nc.vector.tensor_tensor(lbc[:, 0, :], P_("lb0"), P_("lb1"), ALU.max))
            here(nc.vector.tensor_tensor(lbc[:, 1, :], P_("lb0"), lbc[:, 0, :], ALU.subtract))
            nc.vector.tensor_tensor(lbc[:, 2, :], P_("lb1"), lbc[:, 0, :], ALU.subtract).then_inc(SH["lbm"], 1)
            dve.wait_ge(misc_in, 16)
            here(nc.vector.tensor_copy(ang[:, :], pos_i[:, :]))
            here(nc.vector.tensor_scalar(ang[:, :], ang[:, :], C_("inv_freq"), None, ALU.mult))
            here(nc.vector.tensor_scalar(turn_[:, :], ang[:, :], 1.0 / (2 * math.pi), 12582912.0, ALU.mult, ALU.add))
            here(nc.vector.tensor_scalar(turn_[:, :], turn_[:, :], 12582912.0, None, ALU.subtract))
            c1 = 6.28125
            c2 = float(np.float32(np.round((2 * math.pi - c1) * 2 ** 20) / 2 ** 20))
            c3 = 2 * math.pi - c1 - c2
            for cc in (c1, c2, c3):
                here(nc.vector.scalar_tensor_tensor(ang[:, :], turn_[:, :], -cc, ang[:, :], ALU.mult, ALU.add))
            here(nc.vector.tensor_scalar(red[:, :], ang[:, :], 3.1415925, -3.1415925, ALU.min, ALU.max))
            nc.vector.scalar_tensor_tensor(turn_[:, :], red[:, :], -1.0, red[:, :], ALU.mult, ALU.min).then_inc(S1["trig"], 1)
            dve.wait_ge(S1["trig"], 1)
            nc.vector.tensor_scalar(turn_[:, :], turn_[:, :], math.pi / 2, None, ALU.add).then_inc(S1["trig"], 1)

            def ada_turn(i):
                for cb in range(2):
                    if not is_first(i):
                        dve.wait_ge(ada_mm, i * 2 + cb - 1)
                    for k in range(DT):
                        n = cb * DT + k
                        ada_step(ada_acc[:, cb, :, :], n % RING, 16 * (n // RING + 1) + i * (16 * 2 * DT // RING),
                                 i * 2 * DT + n - 1, k)
                    if not (is_first(i) and cb == 0):
                        ada_result(i * 2 + cb - 1)
            turns(dve, ADA_FIRST // 2, ada_turn)
            ada_result(ADA_FIRST - 1)
            dve.wait_ge(ada_out, ADA_FIRST)
            M = lambda k: mod[:, k * DT:(k + 1) * DT]
            link(nc.vector.scalar_tensor_tensor(coef[:, 0, :], M(1), 1.0, P_("g_pre_mix"), ALU.add, ALU.mult))
            dve.wait_ge(SH["lbe"], 1)
            here(nc.vector.tensor_tensor(lbc[:, 3, :], lbc[:, 1, :], lbc[:, 2, :], ALU.add))
            here(nc.vector.reciprocal(lbc[:, 3, :], lbc[:, 3, :]))
            here(nc.vector.tensor_tensor(lbc[:, 4, :], lbc[:, 1, :], lbc[:, 3, :], ALU.mult))
            here(nc.vector.tensor_scalar(lbc[:, 5, :], lbc[:, 4, :], -1.0, 1.0, ALU.mult, ALU.add))
            dve.wait_ge(S1["tab"], 2)
            here(nc.vector.tensor_scalar(cosq[:, :], cosk[:, :], HD1 ** -0.5, None, ALU.mult))
            here(nc.vector.tensor_scalar(sinq[:, :], sink_[:, :], HD1 ** -0.5, None, ALU.mult))

            if live:
                split_first()
            rsn[0] += 1
            norm_operand(x1, sq1, coef[:, 0, :], M(0))

            if runs("kv"):
                job(J["kv"], lambda i, g: proj[:, KA:KA + 2, :])

                def side(i, p, final):
                    if final and p == 1:
                        here(nc.vector.tensor_tensor(kr[:, :], proj[:, KA, :], cosk[:, :], ALU.mult))
                        dve.wait_ge(S1["swap"], 1)
                        here(nc.vector.tensor_tensor(ang[:, :], pss[:, 0, 0:S], sink_[:, :], ALU.mult))
                        nc.vector.tensor_tensor(kr[:, :], kr[:, :], ang[:, :], ALU.add).then_inc(S1["kr"], 1)
                job(J["qa"], lambda i, g: proj[:, ds(4 * i + 2 * g, 2), :], None, side)

            if runs("hg"):
                SN = 7
                sn = [0]

                def side(b, p, final):
                    if p == 0:
                        sn[0] = 0

                    def step(ins):
                        ins.then_inc(S1["step"], 1)
                        sn[0] += 1
                        dve.wait_ge(S1["step"], b * SN + sn[0])
                    sk = par[:, ds(4 * b + PAR["sinks"][0], 4)]
                    if p == 1:
                        q2 = proj[:, ds(2 * b, 2), :]
                        step(nc.vector.tensor_tensor(q_cos[:, :, :], q2, mid(cosq[:, :], 2), ALU.mult))
                        dve.wait_ge(S1["qswap"], b + 1)
                        step(nc.vector.tensor_tensor(q_sin[:, :, :], pss[:, 1, :].rearrange("p (a s) -> p a s", a=2),
                                                     mid(sinq[:, :], 2), ALU.mult))
                        nc.vector.tensor_tensor(qr[:, :, :], q_cos[:, :, :], q_sin[:, :, :], ALU.add).then_inc(S1["qr"], 1)
                    if p == 5:
                        dve.wait_ge(S1["s"], b + 1)
                        nc.vector.tensor_reduce(mx[:, 0, :], pss[:, :, 0:P], AX.X, ALU.max)
                        step(nc.vector.tensor_reduce(mx[:, 1, :], pss[:, :, P:3 * P], AX.X, ALU.max))
                        step(nc.vector.tensor_tensor(mx1[:, :, :], mx[:, :, :], mid(sk, 2), ALU.max))
                        step(nc.vector.tensor_scalar(negm[:, :, :], mx1[:, :, :], -1.0, None, ALU.mult))
                        nc.vector.tensor_tensor(es[:, :, :], negm[:, :, :], mid(sk, 2), ALU.add).then_inc(S1["mx"], 1)
                    if p == 8:
                        dve.wait_ge(S1["es"], b + 1)
                        step(nc.vector.tensor_tensor(den[:, :, :], den[:, :, :], es[:, :, :], ALU.add))
                        step(nc.vector.reciprocal(den[:, :, :], den[:, :, :]))
                        nc.vector.tensor_tensor(probs[:, :, 0:P], probs[:, :, 0:P], last(den[:, 0, :], P), ALU.mult)
                        nc.vector.tensor_tensor(probs[:, :, P:3 * P], probs[:, :, P:3 * P], last(den[:, 1, :], 2 * P),
                                                ALU.mult).then_inc(S1["pn"], 1)
                    if p == 15:
                        dve.wait_ge(S1["hi"], b + 1)
                        nc.vector.tensor_tensor(attn_x[:, ds(2 * b, 2), S:2 * S], pss[:, 0, :].rearrange("p (a s) -> p a s", a=2),
                                                attn_x[:, ds(2 * b, 2), 0:S].bitcast(F32), ALU.subtract).then_inc(S1["lo"], 1)
                        assert sn[0] == SN, sn

                def after(i, g):
                    if g == 1:
                        dve.wait_ge(SH["act"], 3 * i + 2)
                        for a in range(2):
                            t = proj[:, ds(2 * i + FH + a, 1), :]
                            ins = nc.vector.tensor_scalar(t, t, lbc[:, 5, ds(2 * i + a, 1)], lbc[:, 4, ds(2 * i + a, 1)],
                                                          ALU.mult, ALU.add)
                        ins.then_inc(SH["prep"], 1)
                job(J["hg"], lambda i, g: proj[:, ds((QH, FH, IH, GH)[g] + 2 * i, 2), :], after, side, ada_acc2)

            if runs("m1"):
                dve.wait_ge(SH["act"], 12)
                dve.wait_ge(level_ld, 16)
                cum = decay[:, 6, :]
                PER = 4
                k = [0]

                def side(i, p, final):
                    h, q = 2 * i + p // 6, p % 6
                    if q == 0:
                        k[0] = 0

                    def step(ins):
                        ins.then_inc(hl, 1)
                        k[0] += 1
                        dve.wait_ge(hl, h * PER + k[0])
                    if q == 0:
                        f = proj[:, ds(FH + h, 1), :].rearrange("p a s -> p (a s)")
                        dve.wait_ge(SH["o"], h + 1)
                        nc.vector.tensor_scalar(hg_k[:, :], f, -1.0, 1.0, ALU.mult, ALU.add)
                        dve.wait_ge(SH["ln"], h + 1)
                        step(nc.vector.tensor_tensor_scan(cum, C_("chunk_scan"), hg_l[:, :], 0.0, ALU.mult, ALU.add))
                        for n, m in enumerate(LEVELS):
                            b4 = cum.rearrange("p (n t m) -> p n t m", t=2, m=m)
                            d4 = decay[:, n, :].rearrange("p (n t m) -> p n t m", t=2, m=m)
                            ref = b4[:, :, 0, m - 1:m].broadcast_to((P, S // (2 * m), m))
                            nc.vector.tensor_tensor(d4[:, :, 1, :], b4[:, :, 1, :], ref, ALU.subtract)
                            nc.vector.tensor_tensor(d4[:, :, 0, :], ref, b4[:, :, 0, :], ALU.subtract)
                        cc = cum.rearrange("p (n m) -> p n m", m=CH)
                        nc.vector.tensor_tensor(decay[:, 7, :].rearrange("p (n m) -> p n m", m=CH),
                                                cc[:, :, CH - 1:CH].broadcast_to((P, S // CH, CH)), cc,
                                                ALU.subtract).then_inc(SH["d"], 1)
                    if q == 2:
                        dve.wait_ge(SH["exp"], h + 1)
                        dve.wait_ge(SH["cp"], 2 * h + 2)
                        nc.vector.tensor_tensor(Pq[:, :, :], decay[:, 0:7, :], mid(hg_q[:, :], 7), ALU.mult)
                        nc.vector.tensor_tensor(Rk[:, 0:6, :], decay[:, 0:6, :], mid(hg_k[:, :], 6), ALU.mult)
                        step(nc.vector.tensor_tensor(Rk[:, 6, :], decay[:, 7, :], hg_k[:, :], ALU.mult))
                        nc.vector.tensor_copy(p_c[:, 0:CH], Pq[:, 6, 2 * CH:3 * CH])
                        nc.vector.tensor_scalar(p_c[:, CH:2 * CH], Pq[:, 6, 3 * CH:4 * CH], decay[:, 6, 3 * CH - 1:3 * CH], None,
                                                ALU.mult)
                        nc.vector.tensor_scalar(r_c[:, 0:CH], Rk[:, 6, 0:CH], decay[:, 6, 2 * CH - 1:2 * CH], None, ALU.mult)
                        nc.vector.tensor_copy(r_c[:, CH:2 * CH], Rk[:, 6, CH:2 * CH]).then_inc(SH["pr"], 1)
                        dve.wait_ge(SH["pr"], h + 1)
                    if q == 4:
                        for a, (s_, m_) in enumerate((("sa", "ma"), ("sb", "mb"))):
                            dve.wait_ge(SH[s_], h + 1 + a)
                            step(nc.vector.tensor_tensor(masked[:, :, :].rearrange("p l s -> p (l s)"),
                                                         pss[:, 2 * a:2 * a + 2, :].rearrange("p t s -> p (t s)"),
                                                         level_mask[:, :], ALU.mult))
                            nc.vector.tensor_reduce(s_ab[:, a, :], masked[:, :, :].rearrange("p l s -> p s l"), AX.X, ALU.add
                                                    ).then_inc(SH[m_], 1)
                            dve.wait_ge(SH[m_], h + 1 + a)
                        dve.wait_ge(SH["mb"], h + 2)
                        assert k[0] == PER - 0, k

                def after(i, g):
                    n = 2 * i + g // 2
                    d = proj[:, ds(2 * n, 2), :]
                    if g % 2 == 0:
                        dve.wait_ge(gate_ready, n + 1)
                        nc.vector.tensor_scalar(d, d, 0.5, 0.5, ALU.mult, ALU.add).then_inc(gate_half, 1)
                    else:
                        dve.wait_ge(gate_half, n + 1)
                        dve.wait_ge(ps_free, sums_done(J["m1"], i, g))
                        nc.vector.tensor_tensor(d, d, u_a[:, :, :], ALU.mult).then_inc(mul_done, 1)
                job(J["m1"], lambda i, g: u_a[:, :, :] if g % 2 else proj[:, ds(4 * i + g, 2), :], after, side)
                dve.wait_ge(SH["rs"], 1)
                here(nc.vector.scalar_tensor_tensor(flat(hfull), flat3(proj[:, IH:IH + 8, :]), P_("hg_norm"), flat(hrs),
                                                    ALU.mult, ALU.mult))
                nc.vector.tensor_tensor(hfull[:, :, :], hfull[:, :, :], proj[:, GH:GH + 8, :], ALU.mult).then_inc(SH["full"], 1)
                dve.wait_ge(SH["hi"], 1)
                nc.vector.tensor_tensor(hgrn_x[:, :, S:2 * S], hfull[:, :, :], hgrn_x[:, :, 0:S].bitcast(F32), ALU.subtract
                                        ).then_inc(SH["lo"], 1)

            if runs("m2"):
                dve.wait_ge(mul_done, 8)

                def after(i, g):
                    if g % 2 == 0:
                        return
                    n = 2 * i + g // 2
                    dve.wait_ge(gate_ready, n + 9)
                    dve.wait_ge(ps_free, sums_done(J["m2"], i, g))
                    nc.vector.tensor_tensor(u_h[:, :, :], u_h[:, :, :], t_h[:, :, :], ALU.mult).then_inc(mul_done, 1)
                    dve.wait_ge(mul_done, n + 9)
                    nc.vector.tensor_tensor(full[:, :, :], u_h[:, :, :], proj[:, ds(2 * n, 2), :], ALU.add).then_inc(full_ready, 1)
                    dve.wait_ge(fhi_ready, n + 1)
                    nc.vector.tensor_tensor(merged[:, ds(2 * n, 2), S:2 * S], full[:, :, :],
                                            merged[:, ds(2 * n, 2), 0:S].bitcast(F32), ALU.subtract).then_inc(opnd_ready, 1)
                job(J["m2"], lambda i, g: (u_h if g % 2 else t_h)[:, :, :], after)

            def residual(dst, coefs, k, first):
                rsn[0] += 1
                dve.wait_ge(rs_ready, rsn[0])
                for q in range(4):
                    t = slice(4 * q, 4 * q + 4)
                    here(nc.vector.tensor_tensor(y[:, t, :], y[:, t, :], mid(rstd[:, :], 4), ALU.mult))
                    for a in range(4):
                        n = 4 * q + a
                        ins = nc.vector.scalar_tensor_tensor(x_res[:, n, :], y[:, n, :], coefs[:, n:n + 1], x_res[:, n, :],
                                                             ALU.mult, ALU.add)
                    ins.then_inc(y_ready, 1)
                dve.wait_ge(y_ready, 4 * k)

            def to_y(step, per):
                return lambda i, g: y[:, ds(step * i + 2 * g, 2), :]

            if runs("out"):
                job(J["out"], to_y(8, 4), acc=ada_acc3)
                dve.wait_ge(ada_out, J["out"].m0 + 2)
                here(nc.vector.scalar_tensor_tensor(coef[:, 1, :], M(4), 1.0, P_("g_pre_ffn"), ALU.add, ALU.mult))
                here(nc.vector.tensor_tensor(coef[:, 2, :], M(2), P_("g_post_mix"), ALU.mult))
                dve.wait_ge(x_back, 16)
                residual(x_res, coef[:, 2, :], 1, True)
                rsn[0] += 1
                norm_operand(x_res, sq, coef[:, 1, :], M(3))

            def swiglu(j, k0, g0):
                def after(i, g):
                    if g == 1:
                        dve.wait_ge(gate_ready, g0 + i + 1)
                        dve.wait_ge(ps_free, sums_done(j, i, g))
                        nc.vector.tensor_tensor(fullf[:, :, :], t_u[:, :, :], sg[:, :, :], ALU.mult).then_inc(full_ready, 1)
                        dve.wait_ge(fhi_ready, k0 + i + 1)
                        nc.vector.tensor_tensor(hid[:, ds(2 * i, 2), S:2 * S], fullf[:, :, :],
                                                hid[:, ds(2 * i, 2), 0:S].bitcast(F32), ALU.subtract).then_inc(opnd_ready, 1)
                return after

            def add_y(j, dst):
                def after(i, g):
                    dve.wait_ge(ps_free, sums_done(j, i, g))
                    d = dst[:, ds(2 * (len(j.groups) * i + g), 2), :]
                    nc.vector.tensor_tensor(d, d, t_g[:, :, :], ALU.add).then_inc(add_done, 1)
                    dve.wait_ge(add_done, addn[j.name] + i * len(j.groups) + g + 1)
                return after
            addn = {"dn1b": 0, "out2": 8, "dn2b": 16}

            if runs("up1a"):
                job(J["up1a"], lambda i, g: (t_g, t_u)[g][:, :, :], swiglu(J["up1a"], 8, 16))
                job(J["dn1a"], to_y(8, 4), acc=ada_acc4)
                dve.wait_ge(ada_out, J["dn1a"].m0 + 2)
                here(nc.vector.tensor_tensor(coef[:, 3, :], M(5), P_("g_post_ffn"), ALU.mult))
                job(J["up1b"], lambda i, g: (t_g, t_u)[g][:, :, :], swiglu(J["up1b"], 20, 28))
                job(J["dn1b"], lambda i, g: t_g[:, :, :], add_y(J["dn1b"], y))
                residual(x_res, coef[:, 3, :], 2, False)
                rsn[0] += 1
                norm_operand(x_res, sq, P_("attn_norm_g_2"), None)

            if runs("in2"):
                job(J["in2"], lambda i, g: proj2[:, ds(4 * i + 2 * g, 2), :])

                def side(i, p, final):
                    if p == 1 and i == 0:
                        dve.wait_ge(S2["row"], 1)
                        nc.vector.memset(bias_row[0:HEADS2, S:], NEG).then_inc(S2["rowo"], 1)
                        nc.vector.tensor_copy(bias_row[0:HEADS2, 0:S], pss[0:HEADS2, 0, 0:S]).then_inc(S2["rowo"], 1)
                        here(nc.vector.tensor_scalar(den2[:, 0, 0:1], P_("q_norm_g_2"), P ** -0.5, None, ALU.mult))
                    if p == 5:
                        dve.wait_ge(S2["rs"], i + 1)
                        dve.wait_ge(ps_free, all_sums(J["in2"]))
                        t8 = proj2[:, 8 * i:8 * i + 8, :]
                        gain = P_("k_norm_g_2") if i else den2[:, 0, 0:1]
                        nc.vector.scalar_tensor_tensor(flat3(t8), flat3(t8), gain, flat3(sq2[:, 8 * i:8 * i + 8, :]),
                                                       ALU.mult, ALU.mult).then_inc(S2["qk"], 1)
                job(J["in2v"], lambda i, g: proj2[:, ds(4 * i + 2 * g + V2, 2), :], None, side)
                dve.wait_ge(S2["qk"], 2)

                def side(b, p, final):
                    if p == 3:
                        dve.wait_ge(S2["s"], b + 1)
                        nc.vector.tensor_reduce(mx2[:, 0, :], pss[:, :, 0:P], AX.X, ALU.max)
                        here(nc.vector.tensor_reduce(mx2[:, 1, :], pss[:, :, P:3 * P], AX.X, ALU.max))
                        nc.vector.tensor_scalar(negm2[:, :, :], mx2[:, :, :], -1.0, None, ALU.mult).then_inc(S2["mx"], 1)
                    if p == 6:
                        dve.wait_ge(S2["e"], 4 * b + 4)
                        here(nc.vector.reciprocal(den2[:, :, :], den2[:, :, :]))
                        nc.vector.tensor_tensor(probs2[:, :, 0:P], probs2[:, :, 0:P], last(den2[:, 0, :], P), ALU.mult)
                        nc.vector.tensor_tensor(probs2[:, :, P:3 * P], probs2[:, :, P:3 * P], last(den2[:, 1, :], 2 * P),
                                                ALU.mult).then_inc(S2["pn"], 1)
                job(J["in2p"], lambda i, g: proj2[:, ds(4 * i + 2 * g + P2, 2), :], None, side)
                dve.wait_ge(level_ld, 32)
                dve.wait_ge(ps_free, all_sums(J["in2p"]))
                for g in (2, 3):
                    ins = pooled(nc.vector, here, g, dve_pads)
                    if g == 2:
                        here(ins)
                ins.then_inc(S2["mix"], 1)
                dve.wait_ge(S2["hi"], 1)
                nc.vector.tensor_tensor(X[:, 0:8, S:2 * S], proj2[:, V2:V2 + 8, :], X[:, 0:8, 0:S].bitcast(F32), ALU.subtract
                                        ).then_inc(S2["lo"], 1)
                dve.wait_ge(S2["phi"], 1)
                nc.vector.tensor_tensor(X[:, 8:16, S:2 * S], pful[:, :, :], X[:, 8:16, 0:S].bitcast(F32), ALU.subtract
                                        ).then_inc(S2["plo"], 1)
            if runs("out2"):
                job(J["out2"], lambda i, g: t_g[:, :, :], add_y(J["out2"], x_res))
                rsn[0] += 1
                norm_operand(x_res, sq, P_("ffn_norm_g_2"), None)

            def conv(j, k0, f0, g0):
                def after(i, g):
                    t0 = (24 if j.name == "up2b" else 0) + (HIDT if g else 0)
                    n = 4 * (k0 + i) + 2 * g
                    for tap_ in (1, 0):
                        for a in range(2):
                            if tap_ == 1:
                                dve.wait_ge(SC["aff"], n + a + 1)
                            o = PAR["conv_w_2"][0] + tap_ * 2 * HIDT + t0 + a
                            ins = nc.vector.scalar_tensor_tensor(cacc[:, g, a, :], cu[:, g, a, tap_:tap_ + CW],
                                                                 par[:, ds(2 * i + o, 1)], cacc[:, g, a, :],
                                                                 ALU.mult, ALU.add)
                            if a == 1 and tap_ == 1:
                                ins.then_inc(cmid, 1)
                                dve.wait_ge(cmid, 2 * (k0 + i) + g + 1)
                    ins.then_inc(SC["acc"], 1)
                    if g == 1:
                        dve.wait_ge(gate_ready, g0 + i + 1)
                        dve.wait_ge(SC["acc"], 2 * (k0 + i) + 2)
                        nc.vector.tensor_tensor(cful[:, :, :], cacc[:, 1, :, :], csg[:, :, :], ALU.mult).then_inc(full_ready, 1)
                        dve.wait_ge(fhi_ready, f0 + i + 1)
                        nc.vector.tensor_tensor(hid[:, ds(2 * i, 2), S:2 * S], cful[:, :, :],
                                                hid[:, ds(2 * i, 2), 0:S].bitcast(F32), ALU.subtract).then_inc(opnd_ready, 1)
                return after
            if runs("up2a"):
                here(nc.vector.memset(cu[:, :, :, 0:2], 0.0))
                job(J["up2a"], lambda i, g: cu[:, g, :, 2:], conv(J["up2a"], 0, 30, 38))
                job(J["dn2a"], to_y(4, 2))
                here(nc.vector.memset(cu[:, :, :, 0:2], 0.0))
                job(J["up2b"], lambda i, g: cu[:, g, :, 2:], conv(J["up2b"], 12, 42, 50))
                job(J["dn2b"], lambda i, g: t_g[:, :, :], add_y(J["dn2b"], y))
                for q in range(4):
                    t = slice(4 * q, 4 * q + 4)
                    nc.vector.tensor_tensor(x_res[:, t, :], x_res[:, t, :], y[:, t, :], ALU.add).then_inc(y_ready, 1)

        @block.tensor
        def _(pe):
            def mm(out_, l, r_, start=True, stop=True):
                return nc.tensor.matmul(out_, l, r_, start=start, stop=stop)

            def ada_sum(acc, m):
                for t in range(8):
                    for a in range(2):
                        ins = mm(pss[:, 3, 496 + 2 * t:498 + 2 * t], acc[:, a, t * P:(t + 1) * P], ones_r[:, :],
                                 a == 0, a == 1)
                ins.then_inc(ada_mm, 1)

            def job(j, xs, ready=None, side=None, acc=None):
                def turn(i):
                    for p in range(j.n):
                        g, c = j.where[p]
                        b, kt, x, s = bank_of(j, g), j.groups[g][2], xs(g), half_slot(j, p)
                        if c == 0 and group_no(j, 0, g) > 0:
                            pe.wait_ge(ps_free, sums_done(j, i, g) - 2)
                        if ready and is_first(i):
                            ready(g, c)
                        pe.wait_ge(raw_used, landing_of(j, i, p) + 1)
                        for k in range(KC):
                            kk = c * KC + k
                            for t in range(2):
                                hi = w_hi[:, s, k, t * P:(t + 1) * P]
                                lo = w_lo[:, s, k, t * P:(t + 1) * P]
                                o = psg[:, b + t, :]
                                if kk < kt - 1:
                                    mm(o, hi, x[:, kk, :], kk == 0, False)
                                    ins = mm(o[:, 0:S], lo, x[:, kk, 0:S], False, False)
                                else:
                                    mm(o[:, 0:S], lo, x[:, kk, 0:S], False, False)
                                    ins = mm(o, hi, x[:, kk, :], False, True)
                        ins.then_inc(pe_chunk, 1)
                        if side:
                            side(i, p)
                        if j.ada and p == 2 and not is_first(i):
                            ada_block(j.m0 + i - 1)

                def ada_block(m):
                    pe.wait_ge(ada_split, m + 1)
                    pe.wait_ge(ada_out, m)
                    ada_sum(acc, m)
                turns(pe, j.iters, turn)
                if j.ada:
                    ada_block(j.m0 + j.iters - 1)

            nrm = [0]

            def early_sum(j, sqb):
                def side(i, p):
                    if i == 1 and p == j.n // 2:
                        norm_sum(sqb, (0, 1))
                    if i == 1 and p == j.n - 2:
                        norm_sum(sqb, (2,))
                return side

            def norm_sum(sqb, qs=range(4)):
                pe.wait_ge(ones_set, 1)
                for q in qs:
                    pe.wait_ge(sq_ready, 4 * nrm[0] + q + 1)
                    for a in range(4):
                        t = 4 * q + a
                        ins = mm(pss[:, 0, 0:S], ones[:, :], sqb[:, t, :], t == 0, t == DT - 1)
                if qs[-1] == 3:
                    ins.then_inc(ss_ready, 1)
                    nrm[0] += 1

            nop = [0]

            def x_ready():
                k = nop[0]
                nop[0] += 1

                def ready(g, c):
                    if g == 0 and c < 4:
                        pe.wait_ge(nrm_out, 4 * k + c + 1)
                return ready

            norm_sum(sq1)

            def ada_turn(i):
                for cb in range(2):
                    m = i * 2 + cb
                    pe.wait_ge(ada_split, m + 1)
                    if not (is_first(i) and cb == 0):
                        pe.wait_ge(ada_out, m)
                    ada_sum(ada_hl[:, cb, :, :], m)
            pe.wait_ge(rs_ready, 1)
            pe.wait_ge(ones_set, 2)
            turns(pe, ADA_FIRST // 2, ada_turn)
            pe.sem_inc(S1["pv"], 1)
            pe.sem_inc(SH["sb"], 1)
            pe.sem_inc(SH["o"], 1)
            if runs("kv"):
                pe.wait_ge(con_in, 16)
                pe.wait_ge(ones_set, 3)
                job(J["kv"], lambda g: X, x_ready())

                def side(i, p):
                    if is_first(i):
                        return
                    if p == 0:
                        mm(pss[:, 0, 0:S], C_("rope_swap"), proj[:, KA, :]).then_inc(S1["swap"], 1)
                        for a in range(2):
                            ins = nc.tensor.transpose(pss[:, 2, a * P:(a + 1) * P], proj[:, VA, a * P:(a + 1) * P], C_("ident"))
                        ins.then_inc(S1["vt"], 1)
                    if p == 2:
                        pe.wait_ge(S1["kr"], 1)
                        for g in range(2):
                            mm(pss[:, 1, g * S:(g + 1) * S], C_("kv_pick", g * P, (g + 1) * P), kr[:, :]).then_inc(S1["dup"], 1)
                job(J["qa"], lambda g: X, None, side)
            if runs("hg"):
                pe.wait_ge(S1["dupo"], 1)
                pe.wait_ge(S1["vo"], 1)

                def side(b, p):
                    if p == 0:
                        mm(pss[:, 1, :], C_("rope_swap"), proj[:, ds(2 * b, 2), :].rearrange("p a s -> p (a s)")
                           ).then_inc(S1["qswap"], 1)
                    if p == 4:
                        pe.wait_ge(ada_out, b + J["hg"].m0)
                        pe.wait_ge(S1["lo"], b + 1)
                        pe.wait_ge(S1["qr"], b + 1)
                        pe.wait_ge(S1["kv_now"], b + 1)
                        for hh in range(4):
                            rows = slice(HD1 * (hh % 2), HD1 * (hh % 2) + HD1)
                            for a, (lo_, hi_) in enumerate(((0, P), (P, 3 * P))):
                                o = pss[:, hh, lo_:hi_]
                                mm(o, ident_bf[:, :], band_bf[:, lo_:hi_], True, False)
                                ins = mm(o, qr[rows, hh // 2, a * P:(a + 1) * P], kd_now[rows, 0:hi_ - lo_], False, True)
                        ins.then_inc(S1["s"], 1)
                    if p == 11:
                        pe.wait_ge(S1["pn"], b + 1)
                        for hh in range(4):
                            for a in range(3):
                                ins = nc.tensor.transpose(pss[:, hh, a * P:(a + 1) * P], probs[:, hh, a * P:(a + 1) * P],
                                                          C_("ident"))
                        ins.then_inc(S1["pt"], 1)
                    if p == 13:
                        pe.wait_ge(S1["pto"], b + 1)
                        for hh in range(4):
                            r0 = HD1 * (hh % 2)
                            o = pss[r0:r0 + HD1, 0, (hh // 2) * S:(hh // 2 + 1) * S]
                            v0, v1 = (v_now[:, a, :] for a in range(2))
                            mm(o[:, 0:P], v0, probs_t[:, hh, 0:P])
                            mm(o[:, P:S], v0, probs_t[:, hh, P:2 * P], True, False)
                            ins = mm(o[:, P:S], v1, probs_t[:, hh, 2 * P:3 * P], False, True)
                        ins.then_inc(S1["pv"], 1)
                job(J["hg"], lambda g: X, None, side, ada_hl2)
            if runs("m1"):
                pe.wait_ge(S1["lo"], 5)
                pe.wait_ge(ada_out, J["hg"].m0 + 4)

                def side(i, p):
                    h, q = 2 * i + p // 6, p % 6
                    if q == 1:
                        pe.wait_ge(SH["cp"], 2 * h + 2)
                        pe.wait_ge(SH["oo"], h + 1)
                        for a in range(2):
                            ins = nc.tensor.transpose(pss[:, 0, a * P:(a + 1) * P], hg_v[:, a * P:(a + 1) * P], C_("ident"))
                        ins.then_inc(SH["vt"], 1)
                    if q == 3:
                        pe.wait_ge(SH["vo"], h + 1)
                        pe.wait_ge(SH["pr"], h + 1)
                        for a, s_ in enumerate(("sa", "sb")):
                            c = slice(a * P, (a + 1) * P)
                            for n in range(8):
                                l, r_ = (Rk[:, n, c], Pq[:, n, c]) if n < 7 else (hg_k[:, c], hg_q[:, c])
                                ins = mm(pss[:, 2 * a + n // 4, (n % 4) * P:(n % 4 + 1) * P], l, r_)
                            ins.then_inc(SH[s_], 1)
                    if q == 5:
                        pe.wait_ge(SH["ma"], h + 1)
                        mm(pss[:, 0, 0:P], r_c[:, :], p_c[:, :]).then_inc(SH["sc"], 1)
                        pe.wait_ge(SH["sco"], h + 1)
                        pe.wait_ge(SH["mb"], h + 2)
                        mm(pss[:, 2, 0:P], v_rows[:, 0, :], s_ab[:, 0, :])
                        mm(pss[:, 2, P:S], v_rows[:, 0, :], s_c[:, :], True, False)
                        mm(pss[:, 2, P:S], v_rows[:, 1, :], s_ab[:, 1, :], False, True).then_inc(SH["o"], 1)

                job(J["m1"], lambda g: attn_x if g % 2 else X, None, side)
                pe.wait_ge(SH["oo"], HGH + 1)
                pe.wait_ge(SH["sq"], 1)
                for n in range(4):
                    ins = mm(pss[:, n, :], ones[:, :], hsq[:, 2 * n:2 * n + 2, :].rearrange("p a s -> p (a s)"))
                ins.then_inc(SH["ss"], 1)
            if runs("m2"):
                def ready(g, c):
                    if (g, c) == (1, 0):
                        pe.wait_ge(SH["lo"], 1)
                job(J["m2"], lambda g: hgrn_x if g % 2 else X, ready)

            def operand_ready(k0):
                def ready(g, c):
                    if g == 0:
                        pe.wait_ge(opnd_ready, k0 + 2 * c + 2)
                return ready
            if runs("out"):
                pe.wait_ge(SH["rs"], 1)
                job(J["out"], lambda g: merged, operand_ready(0), early_sum(J["out"], sq_mix), ada_hl3)
                pe.wait_ge(ada_out, J["out"].m0 + 2)
                norm_sum(sq_mix, (3,))
                pe.wait_ge(rs_ready, nrm[0])
                norm_sum(sq)
            if runs("up1a"):
                job(J["up1a"], lambda g: X, x_ready())
                job(J["dn1a"], lambda g: hid, operand_ready(8), None, ada_hl4)
                job(J["up1b"], lambda g: X)
                job(J["dn1b"], lambda g: hid, operand_ready(20), early_sum(J["dn1b"], sq_ffn))
                norm_sum(sq_ffn, (3,))
                pe.wait_ge(rs_ready, nrm[0])
                norm_sum(sq)
            if runs("in2"):
                job(J["in2"], lambda g: X, x_ready())

                def side(i, p):
                    if p == 0 and i == 0:
                        pe.wait_ge(misc_in, 48)
                        mm(pss[0:HEADS2, 0, 0:S], relb[0:BUCKETS, :], hot[0:BUCKETS, :]).then_inc(S2["row"], 1)
                    if p == 2:
                        if i == 0:
                            pe.wait_ge(S2["rowo"], 2)
                        else:
                            pe.wait_ge(S2["rs"], 1)
                        pe.wait_ge(S2["sq"], i + 1)
                        for n in range(4):
                            t = 8 * i + 2 * n
                            ins = mm(pss[:, n, :], ones[:, :], sq2[:, t:t + 2, :].rearrange("p a s -> p (a s)"))
                        ins.then_inc(S2["ss"], 1)
                job(J["in2v"], lambda g: X, None, side)

                def weighted_values(b):
                    pe.wait_ge(S2["pto"], b + 1)
                    for hh in range(4):
                        h = 4 * b + hh
                        o = pss[:, hh // 2, (hh % 2) * S:(hh % 2 + 1) * S]
                        v0, v1 = (v2_rows[:, a, h, :] for a in range(2))
                        mm(o[:, 0:P], v0, probs2_t[:, hh, 0:P])
                        mm(o[:, P:S], v0, probs2_t[:, hh, P:2 * P], True, False)
                        ins = mm(o[:, P:S], v1, probs2_t[:, hh, 2 * P:3 * P], False, True)
                    ins.then_inc(S2["pv"], 1)

                def side(b, p):
                    if p == 0 and b == 0:
                        pe.wait_ge(S2["rs"], 2)
                        pe.wait_ge(ps_free, all_sums(J["in2v"]))
                        for a in range(2):
                            for h in range(8):
                                n = a * 8 + h
                                ins = nc.tensor.transpose(pss[:, n // 4, (n % 4) * P:(n % 4 + 1) * P],
                                                          proj2[:, V2 + h, a * P:(a + 1) * P], C_("ident"))
                        ins.then_inc(S2["vt"], 1)
                    if p == 0 and b == 1:
                        weighted_values(0)
                    if p == 2:
                        if b == 0:
                            pe.wait_ge(S2["vo"], 1)
                            pe.wait_ge(S2["qk"], 2)
                            pe.wait_ge(S2["hk"], 16)
                        else:
                            pe.wait_ge(S2["ao"], 1)
                        for hh in range(4):
                            h = 4 * b + hh
                            for a, (lo_, hi_) in enumerate(((0, P), (P, 3 * P))):
                                o = pss[:, hh, lo_:hi_]
                                mm(o, C_("flip"), hank[:, h, P * (1 - a):S], True, False)
                                ins = mm(o, proj2[:, Q2 + h, a * P:(a + 1) * P], proj2[:, K2 + h, 0:hi_ - lo_], False, True)
                        ins.then_inc(S2["s"], 1)
                    if p == 7:
                        pe.wait_ge(S2["pn"], b + 1)
                        for hh in range(4):
                            for a in range(3):
                                ins = nc.tensor.transpose(pss[:, hh, a * P:(a + 1) * P], probs2[:, hh, a * P:(a + 1) * P],
                                                          C_("ident"))
                        ins.then_inc(S2["pt"], 1)
                job(J["in2p"], lambda g: X, None, side)
                weighted_values(1)
                pe.wait_ge(S2["ao"], 2)
                pe.wait_ge(S2["mix"], 1)
                pe.wait_ge(S2["mixp"], 2)
                pe.wait_ge(S2["pw"], 16)
                for g in range(4):
                    for n in range(2):
                        for k in range(2):
                            ins = mm(pss[:, g, n * S:(n + 1) * S], pwt[:, g, k, n * P:(n + 1) * P], proj2[:, P2 + 2 * g + k, :],
                                     k == 0, k == 1)
                ins.then_inc(S2["pwm"], 1)
            if runs("out2"):
                def ready(g, c):
                    if (g, c) == (0, 0):
                        pe.wait_ge(S2["lo"], 1)
                    if (g, c) == (0, 2):
                        pe.wait_ge(S2["plo"], 1)
                job(J["out2"], lambda g: X, ready)
                norm_sum(sq)
            if runs("up2a"):
                job(J["up2a"], lambda g: X, x_ready())
                job(J["dn2a"], lambda g: hid, operand_ready(30))
                job(J["up2b"], lambda g: X)
                job(J["dn2b"], lambda g: hid, operand_ready(42))


def kernel(**inputs):
    import concourse.bacc as _bacc
    from concourse import mybir as _mybir
    from concourse.bass_utils import run_bass_kernel_spmd as _run

    f = {k: np.asarray(v) for k, v in inputs.items()}

    def cols(a, t):
        return np.ascontiguousarray(a.reshape(t, P).T)

    packed = {
        "c": cols(f["c"][0], DT), "b_ada": cols(f["b_ada"][0], 6 * DT), "g_pre_mix": cols(f["g_pre_mix"][0], DT),
        "g_post_mix": cols(f["g_post_mix"][0], DT), "g_pre_ffn": cols(f["g_pre_ffn"][0], DT),
        "g_post_ffn": cols(f["g_post_ffn"][0], DT), "sinks": np.broadcast_to(f["attn_sinks"][0], (P, HEADS1)),
        "lb0": cols(f["hg_lower_bounds"][0], HGH), "lb1": cols(f["hg_lower_bounds"][1], HGH),
        "hg_norm": cols(f["hg_norm"][0], 1), "attn_norm_g_2": cols(f["attn_norm_g_2"][0], DT),
        "q_norm_g_2": cols(f["q_norm_g_2"][0], 1), "k_norm_g_2": cols(f["k_norm_g_2"][0], 1),
        "pool_scale_2": cols(f["pool_scale_2"][0], 8), "ffn_norm_g_2": cols(f["ffn_norm_g_2"][0], DT),
        "conv_w_2": cols(f["conv_w_2"][0], 3 * 2 * HIDT), "conv_b_2": cols(f["conv_b_2"][0], 2 * HIDT),
    }
    con, hot, level_mask, inv_count = constants()
    arrays = {
        "xT": np.ascontiguousarray(f["x"][0].T), "params": np.concatenate([packed[n] for n in PAR], axis=1),
        "cons": con, "level_in": level_mask, "count_in": inv_count, "hot_in": hot, "rel_bias": np.ascontiguousarray(f["rel_bias_2"].T), "pos": f["positions"][0],
        "w_ada": f["w_ada"][0], "w_in": f["w_in"][0], "w_attn": f["w_attn_proj"][0], "w_hgrn": f["w_hgrn_proj"][0],
        "w_out": f["w_out"][0], "w_ffn_in": f["w_ffn_in"][0], "w_ffn_out": f["w_ffn_out"][0], "w_in2": f["w_in_2"][0],
        "pool_w": f["pool_w_2"][0], "w_out2": f["w_out_2"][0], "w_up": f["w_up_2"][0], "w_down": f["w_down_2"][0],
    }
    nc = _bacc.Bacc("TRN2", target_bir_lowering=False, num_devices=1)
    args = {}
    ins = {}
    for name, a in arrays.items():
        a = np.ascontiguousarray(a)
        ins[f"in_{name}"] = a
        args[name] = nc.dram_tensor(f"in_{name}", a.shape, _mybir.dt.from_np(a.dtype), kind="ExternalInput").ap()
    out = nc.dram_tensor("out_T", (D, S), _mybir.dt.float32, kind="ExternalOutput").ap()
    two_block_kernel(nc, out=out, **args)
    r = _run(nc, [ins], core_ids=[0])
    return np.ascontiguousarray(r.results[0]["out_T"].T)[None]
```
